# Optimizing a Trainium2 kernel written in Bass

```python
import jax, jax.numpy as jnp
from jax import lax
import numpy as np

D_MODEL = 1024
BATCH = 1
SEQ = 1024
DEPTH = 1

GRID_W = 64
CTX_LEN = 256
N_MLA_HEADS = 8
MLA_Q_RANK = 256
MLA_KV_RANK = 128
MLA_NOPE_DIM = 64
MLA_ROPE_DIM = 32
MLA_QK_DIM = MLA_NOPE_DIM + MLA_ROPE_DIM
MLA_V_DIM = 64
N_GLA_HEADS = 4
GLA_DK = 64
GLA_DV = 128
GLA_GATE_RANK = 16
GLA_GATE_NORM = 16.0
GLA_CHUNK = 64
D_FF = 2816
MACARON_WEIGHT = 0.5
Q_BLOCK = 128
ROPE_BASE = 10000.0
EPS = 1e-6
N_MOD = 9

D_MLA_OUT = N_MLA_HEADS * MLA_V_DIM
D_GLA_OUT = N_GLA_HEADS * GLA_DV
D_MIX = D_MLA_OUT + D_GLA_OUT
IN_SPLITS = (MLA_Q_RANK, MLA_KV_RANK + MLA_ROPE_DIM, N_GLA_HEADS * GLA_DK, N_GLA_HEADS * GLA_DK,
             D_GLA_OUT, D_GLA_OUT, 2 * GLA_GATE_RANK)
D_IN = 256 + 160 + 256 + 256 + 512 + 512 + 32

kernel_name = "hybrid_mla_gla_macaron_dit_block"

def split_cols(t, sizes):
    out, start = [], 0
    for s in sizes:
        out.append(t[..., start:start + s])
        start += s
    return out

def rmsnorm(x, g):
    xf = x.astype(jnp.float32)
    y = xf * lax.rsqrt(jnp.mean(xf * xf, axis=-1, keepdims=True) + EPS)
    return (y * g.astype(jnp.float32)).astype(x.dtype)

def modulate(h, shift, scale):
    return h * (1 + scale[:, None, :]) + shift[:, None, :]

def ffn_sublayer(x, g_pre, g_post, shift, scale, gate, w_in, w_out):
    h = modulate(rmsnorm(x, g_pre), shift, scale)
    a, b = jnp.split(h @ w_in, 2, axis=-1)
    y = (jax.nn.silu(a) * b) @ w_out
    return x + MACARON_WEIGHT * gate[:, None, :] * rmsnorm(y, g_post)

def axial_rope_angles(n):
    rows = n // GRID_W
    row = jnp.repeat(jnp.arange(rows, dtype=jnp.float32), GRID_W)
    col = jnp.tile(jnp.arange(GRID_W, dtype=jnp.float32), rows)
    axis_dim = MLA_ROPE_DIM // 2
    inv_freq = ROPE_BASE ** (-jnp.arange(0, axis_dim, 2, dtype=jnp.float32) / axis_dim)
    return row[:, None] * inv_freq, col[:, None] * inv_freq

def rotate_axis(x, ang):
    x1, x2 = jnp.split(x, 2, axis=-1)
    cos, sin = jnp.cos(ang), jnp.sin(ang)
    return jnp.concatenate([x1 * cos - x2 * sin, x2 * cos + x1 * sin], axis=-1)

def apply_rope_2d(x, ang_row, ang_col):
    xr, xc = jnp.split(x.astype(jnp.float32), 2, axis=-1)
    return jnp.concatenate([rotate_axis(xr, ang_row), rotate_axis(xc, ang_col)], axis=-1).astype(x.dtype)

def gla_log_decay(a_low, w_b, b_b):
    b, t, _ = a_low.shape
    la = jax.nn.log_sigmoid((a_low @ w_b + b_b).astype(jnp.float32)) / GLA_GATE_NORM
    return la.reshape(b, t, N_GLA_HEADS, GLA_DK)

def mixer_inputs(h, p, angles=None):
    b, t, _ = h.shape
    q_a, kv_a, gq, gk, gv, gg, ga = split_cols(h @ p["w_in"], IN_SPLITS)
    q = (rmsnorm(q_a, p["mla_q_norm"]) @ p["mla_w_qb"]).reshape(b, t, N_MLA_HEADS, MLA_QK_DIM)
    q_nope, q_rope = q[..., :MLA_NOPE_DIM], q[..., MLA_NOPE_DIM:]
    kv = (rmsnorm(kv_a[..., :MLA_KV_RANK], p["mla_kv_norm"]) @ p["mla_w_kvb"]).reshape(
        b, t, N_MLA_HEADS, MLA_NOPE_DIM + MLA_V_DIM)
    k_nope, v = kv[..., :MLA_NOPE_DIM], kv[..., MLA_NOPE_DIM:]
    k_rope = kv_a[..., MLA_KV_RANK:]
    if angles is not None:
        ang_row, ang_col = angles
        q_rope = apply_rope_2d(q_rope, ang_row[:, None, :], ang_col[:, None, :])
        k_rope = apply_rope_2d(k_rope, ang_row, ang_col)
    q = jnp.concatenate([q_nope, q_rope], axis=-1)
    k = jnp.concatenate(
        [k_nope, jnp.broadcast_to(k_rope[:, :, None, :], (b, t, N_MLA_HEADS, MLA_ROPE_DIM))], axis=-1)
    gla = (gq.reshape(b, t, N_GLA_HEADS, GLA_DK) * (GLA_DK ** -0.5),
           gk.reshape(b, t, N_GLA_HEADS, GLA_DK),
           gv.reshape(b, t, N_GLA_HEADS, GLA_DV),
           gg,
           gla_log_decay(ga[..., :GLA_GATE_RANK], p["gla_w_a_fwd"], p["gla_b_a_fwd"]),
           gla_log_decay(ga[..., GLA_GATE_RANK:], p["gla_w_a_bwd"], p["gla_b_a_bwd"]))
    return q, k, v, gla

def softmax_attend(q, k, v):
    s = jnp.einsum('bqhd,bkhd->bhqk', q, k).astype(jnp.float32) * (MLA_QK_DIM ** -0.5)
    probs = jax.nn.softmax(s, axis=-1).astype(v.dtype)
    return jnp.einsum('bhqk,bkhd->bqhd', probs, v)

def blocked_attend(q, k, v):
    b, n, h, d = q.shape
    nb = n // Q_BLOCK
    qb = jnp.moveaxis(q.reshape(b, nb, Q_BLOCK, h, d), 1, 0)
    out = lax.map(lambda blk: softmax_attend(blk, k, v), qb)
    return jnp.moveaxis(out, 0, 1).reshape(b, n, h, v.shape[-1])

def gla_chunked(q, k, v, log_a, s0):
    b, t, h, dk = q.shape
    dv = v.shape[-1]
    nc = t // GLA_CHUNK

    def to_chunks(a):
        return a.reshape(b, nc, GLA_CHUNK, h, a.shape[-1]).transpose(1, 0, 3, 2, 4)

    lower = jnp.tril(jnp.ones((GLA_CHUNK, GLA_CHUNK), dtype=bool))

    def step(state, inp):
        qc, kc, vc, gc = inp
        qc, kc, vc = qc.astype(jnp.float32), kc.astype(jnp.float32), vc.astype(jnp.float32)
        cum = jnp.cumsum(gc, axis=-2)
        o_inter = jnp.einsum('bhcd,bhde->bhce', qc * jnp.exp(cum), state)
        diff = cum[..., :, None, :] - cum[..., None, :, :]
        decay = jnp.exp(jnp.where(lower[:, :, None], diff, -jnp.inf))
        attn = jnp.einsum('bhid,bhjd,bhijd->bhij', qc, kc, decay)
        o_intra = jnp.einsum('bhij,bhje->bhie', attn, vc)
        last = cum[..., -1:, :]
        new_state = jnp.exp(last)[..., 0, :, None] * state + jnp.einsum(
            'bhjd,bhje->bhde', kc * jnp.exp(last - cum), vc)
        return new_state, o_inter + o_intra

    s_final, o = lax.scan(step, s0, (to_chunks(q), to_chunks(k), to_chunks(v), to_chunks(log_a)))
    o = o.transpose(1, 0, 3, 2, 4).reshape(b, t, h, dv)
    return o.astype(v.dtype), s_final

def gla_bidirectional(gq, gk, gv, la_f, la_b, s_f, s_b):
    flip = lambda a: jnp.flip(a, axis=1)
    o_f, s_f_new = gla_chunked(gq, gk, gv, la_f, s_f)
    o_b, s_b_new = gla_chunked(flip(gq), flip(gk), flip(gv), flip(la_b), s_b)
    return o_f + flip(o_b), s_f_new, s_b_new

def gla_output(o, gg, gain):
    b, t = o.shape[:2]
    gate = jax.nn.silu(gg.reshape(b, t, N_GLA_HEADS, GLA_DV))
    return (rmsnorm(o, gain) * gate).reshape(b, t, D_GLA_OUT)

def token_mixing(a_lat, a_ctx, angles, p, need_ctx_out):
    b, n, _ = a_lat.shape
    q_c, k_c, v_c, gla_c = mixer_inputs(a_ctx, p)
    q_l, k_l, v_l, gla_l = mixer_inputs(a_lat, p, angles)
    k_all = jnp.concatenate([k_c, k_l], axis=1)
    v_all = jnp.concatenate([v_c, v_l], axis=1)
    mla_lat = blocked_attend(q_l, k_all, v_all).reshape(b, n, D_MLA_OUT)
    s0 = jnp.zeros((a_ctx.shape[0], N_GLA_HEADS, GLA_DK, GLA_DV), jnp.float32)
    cq, ck, cv, cg, cla_f, cla_b = gla_c
    o_c, s_cf, s_cb = gla_bidirectional(cq, ck, cv, cla_f, cla_b, s0, s0)
    lq, lk, lv, lg, lla_f, lla_b = gla_l
    o_l, _, _ = gla_bidirectional(lq, lk, lv, lla_f, lla_b, s_cf, s_cb)
    gla_lat = gla_output(o_l, lg, p["gla_norm"])
    y_lat = jnp.concatenate([mla_lat, gla_lat], axis=-1) @ p["w_out"]
    if need_ctx_out:
        m = a_ctx.shape[1]
        mla_ctx = softmax_attend(q_c, k_c, v_c).reshape(a_ctx.shape[0], m, D_MLA_OUT)
        gla_ctx = gla_output(o_c, cg, p["gla_norm"])
        y_ctx = jnp.concatenate([mla_ctx, gla_ctx], axis=-1) @ p["w_out"]
    else:
        y_ctx = None
    return y_lat, y_ctx

def setup_inputs(seed: int = 0) -> dict:
    key = jax.random.key(seed)
    ks = jax.random.split(key, 24)
    f32 = jnp.float32
    nrm = lambda k, shape, s: jax.random.normal(k, shape, f32) * s
    L, D = DEPTH, D_MODEL
    return {
        "x": nrm(ks[0], (BATCH, SEQ, D), 1.0),
        "c": nrm(ks[1], (BATCH, D), 1.0),
        "ctx": nrm(ks[2], (BATCH, CTX_LEN, D), 1.0),
        "c_ctx": nrm(ks[3], (D,), 1.0),
        "w_ada": nrm(ks[4], (L, D, N_MOD * D), 0.5 * D ** -0.5),
        "b_ada": nrm(ks[5], (L, N_MOD * D), 0.02),
        "norm_pre": 1.0 + nrm(ks[6], (L, 3, D), 0.05),
        "norm_post": 1.0 + nrm(ks[7], (L, 3, D), 0.05),
        "ffn1_w_in": nrm(ks[8], (L, D, 2 * D_FF), D ** -0.5),
        "ffn1_w_out": nrm(ks[9], (L, D_FF, D), D_FF ** -0.5),
        "ffn2_w_in": nrm(ks[10], (L, D, 2 * D_FF), D ** -0.5),
        "ffn2_w_out": nrm(ks[11], (L, D_FF, D), D_FF ** -0.5),
        "w_in": nrm(ks[12], (L, D, D_IN), D ** -0.5),
        "mla_q_norm": 1.0 + nrm(ks[13], (L, MLA_Q_RANK), 0.05),
        "mla_w_qb": nrm(ks[14], (L, MLA_Q_RANK, N_MLA_HEADS * MLA_QK_DIM), MLA_Q_RANK ** -0.5),
        "mla_kv_norm": 1.0 + nrm(ks[15], (L, MLA_KV_RANK), 0.05),
        "mla_w_kvb": nrm(ks[16], (L, MLA_KV_RANK, N_MLA_HEADS * (MLA_NOPE_DIM + MLA_V_DIM)), MLA_KV_RANK ** -0.5),
        "gla_w_a_fwd": nrm(ks[17], (L, GLA_GATE_RANK, N_GLA_HEADS * GLA_DK), GLA_GATE_RANK ** -0.5),
        "gla_b_a_fwd": nrm(ks[18], (L, N_GLA_HEADS * GLA_DK), 0.1),
        "gla_w_a_bwd": nrm(ks[19], (L, GLA_GATE_RANK, N_GLA_HEADS * GLA_DK), GLA_GATE_RANK ** -0.5),
        "gla_b_a_bwd": nrm(ks[20], (L, N_GLA_HEADS * GLA_DK), 0.1),
        "gla_norm": 1.0 + nrm(ks[21], (L, GLA_DV), 0.05),
        "w_out": nrm(ks[22], (L, D_MIX, D), D_MIX ** -0.5),
    }

def reference(x, c, ctx, c_ctx, w_ada, b_ada, norm_pre, norm_post, ffn1_w_in, ffn1_w_out,
              ffn2_w_in, ffn2_w_out, w_in, mla_q_norm, mla_w_qb, mla_kv_norm, mla_w_kvb,
              gla_w_a_fwd, gla_b_a_fwd, gla_w_a_bwd, gla_b_a_bwd, gla_norm, w_out):
    n = x.shape[1]
    angles = axial_rope_angles(n)
    h_lat, h_ctx = x, ctx
    for l in range(DEPTH):
        last = l == DEPTH - 1
        m_lat = jnp.split(jax.nn.silu(c) @ w_ada[l] + b_ada[l], N_MOD, axis=-1)
        m_ctx = jnp.split((jax.nn.silu(c_ctx) @ w_ada[l] + b_ada[l])[None], N_MOD, axis=-1)
        h_lat = ffn_sublayer(h_lat, norm_pre[l, 0], norm_post[l, 0], m_lat[0], m_lat[1], m_lat[2],
                             ffn1_w_in[l], ffn1_w_out[l])
        h_ctx = ffn_sublayer(h_ctx, norm_pre[l, 0], norm_post[l, 0], m_ctx[0], m_ctx[1], m_ctx[2],
                             ffn1_w_in[l], ffn1_w_out[l])
        p = {"w_in": w_in[l], "mla_q_norm": mla_q_norm[l], "mla_w_qb": mla_w_qb[l],
             "mla_kv_norm": mla_kv_norm[l], "mla_w_kvb": mla_w_kvb[l],
             "gla_w_a_fwd": gla_w_a_fwd[l], "gla_b_a_fwd": gla_b_a_fwd[l],
             "gla_w_a_bwd": gla_w_a_bwd[l], "gla_b_a_bwd": gla_b_a_bwd[l],
             "gla_norm": gla_norm[l], "w_out": w_out[l]}
        a_lat = modulate(rmsnorm(h_lat, norm_pre[l, 1]), m_lat[3], m_lat[4])
        a_ctx = modulate(rmsnorm(h_ctx, norm_pre[l, 1]), m_ctx[3], m_ctx[4])
        y_lat, y_ctx = token_mixing(a_lat, a_ctx, angles, p, not last)
        h_lat = h_lat + m_lat[5][:, None, :] * rmsnorm(y_lat, norm_post[l, 1])
        h_lat = ffn_sublayer(h_lat, norm_pre[l, 2], norm_post[l, 2], m_lat[6], m_lat[7], m_lat[8],
                             ffn2_w_in[l], ffn2_w_out[l])
        if not last:
            h_ctx = h_ctx + m_ctx[5][:, None, :] * rmsnorm(y_ctx, norm_post[l, 1])
            h_ctx = ffn_sublayer(h_ctx, norm_pre[l, 2], norm_post[l, 2], m_ctx[6], m_ctx[7], m_ctx[8],
                                 ffn2_w_in[l], ffn2_w_out[l])
    return h_lat


_drawn_inputs = setup_inputs


def setup_inputs(seed=0):
    import zlib

    import numpy as np

    out = dict(_drawn_inputs(seed))
    spreads = {}
    factors = {'norm_post': 2.913,
     'mla_q_norm': 8.0,
     'mla_kv_norm': 8.0,
     'gla_b_a_fwd': 6.474,
     'gla_b_a_bwd': 6.363,
     'gla_norm': 20.797}
    for name, (base, spread) in spreads.items():
        noise = np.random.default_rng([zlib.crc32(name.encode()), seed]).standard_normal(out[name].shape)
        drawn = base * np.exp(spread * noise) if base else spread * noise
        out[name] = __import__('jax').numpy.asarray(drawn.astype(out[name].dtype))
    for name, factor in factors.items():
        out[name] = (out[name] * factor).astype(out[name].dtype)
    return out
```

```python
from contextlib import ExitStack

import numpy as np

import concourse.bass as bass
from concourse import mybir

P = 128
D = 1024
DK = D // P
LAT = 1024
CTX = 256
TOK = LAT + CTX
FF = 2816
FJ = FF // P
HEADS, NOPE, ROPE, VD = 8, 64, 32, 64
QK = NOPE + ROPE
QRANK, KVRANK = 256, 128
GH, GDK, GDV, GRANK = 4, 64, 128, 16
GRID_W = 64
EPS = 1e-6
GATE_NORM = 16.0
C = 128
NC_LAT, NC_CTX = LAT // C, CTX // C
NC = NC_LAT + NC_CTX
BANK = 512
LEVELS = 7

F32 = mybir.dt.float32
F32R = mybir.dt.float32r
U8 = mybir.dt.uint8
ACT = mybir.ActivationFunctionType
ALU = mybir.AluOpType
AX = mybir.AxisListType

CHUNKS = [(0, 512, 0), (512, 512, 0), (1024, 256, 1)]


def build(nc, x_t, cond, w_ada, b_ada, pre, post, f1_in, f1_out, f2_in, f2_out, w_in, w_a, b_a, g_norm, ident_d, mask_d, w_qb, w_kvb, qk_norm,
          rope_d, w_out, x1_d, x2_d, out):
    with ExitStack() as ctx:
        def sem(name):
            return ctx.enter_context(nc.semaphore(name))

        base = -(-nc.sbuf_base // 32) * 32
        end = nc.sbuf_base + nc.sbuf_bytes_remaining
        plan = {"at": base}

        def put(name, shape, dt, at=None):
            size = int(np.prod(shape[1:])) * (1 if dt == U8 else 4)
            at = plan["at"] if at is None else at
            t = nc.alloc_sbuf_tensor_at(name, list(shape), dt, offset=at)
            plan["at"] = at + -(-size // 32) * 32
            assert plan["at"] <= end, (name, plan["at"] - end)
            return t

        bank = ctx.enter_context(nc.psum_tensor("bank", [P, 8, BANK], F32))

        ones = put("ones", [P, P], F32)
        eps = put("eps", [P, 1], F32)
        mods = put("mods", [P, 9, DK, 2], F32)
        bada_sb = put("bada_sb", [P, 9, DK, 2], F32)
        pre_sb = put("pre_sb", [P, 3, DK, 2], F32)
        post_sb = put("post_sb", [P, 3, DK, 2], F32)
        gain_pre = put("gain_pre", [P, 3, DK, 2], F32)
        gain_post = put("gain_post", [P, 3, DK, 2], F32)
        ident = put("ident", [P, P], F32)
        wa_sb = put("wa_sb", [2 * GRANK, 4, P], F32)
        ba_sb = put("ba_sb", [P, 4], F32)
        gnorm_sb = put("gnorm_sb", [P, 1], F32)
        qk_norm_sb = put("qk_norm_sb", [P, 3], F32)
        mask = put("mask", [P, LEVELS, BANK], U8)
        arena = plan["at"]

        class Ada:
            def __init__(self, n, first, tiles, conds, before, at):
                self.first, self.tiles, self.conds = first, tiles, conds
                self.before, self.after = before, before + tiles * conds
                self.cond = put(f"{n}_cond", [P, 2, D], F32, at=at)
                self.w = put(f"{n}_w", [P, 4, D], F32)
                self.junk = put(f"{n}_junk", [P, 2, D], F32)

        ada_a = Ada("ada_a", 0, 2 * DK, 2, 0, arena + DK * TOK * 4)
        mask_raw = put("mask_raw", [P, LEVELS, C], F32)
        ada_b = Ada("ada_b", 2 * DK, 3 * DK, 2, ada_a.after, arena)
        assert plan["at"] <= arena + DK * TOK * 4

        class Room:
            def stream(self, n, at):
                self.a_hi = put(f"{n}_a_hi", [P, DK, self.tok], F32R, at=at)
                self.a_lo = put(f"{n}_a_lo", [P, DK, self.tok], F32R)

            def norm(self, n, at, rstd=None):
                self.xin = put(f"{n}_xin", [P, DK, BANK], F32, at=at)
                self.sq = put(f"{n}_sq", [P, 4, BANK], F32)
                self.tmp = put(f"{n}_tmp", [P, 2, BANK], F32)
                self.rstd = rstd or put(f"{n}_rstd", [P, 2, BANK], F32)

            def hidden(self, n, at):
                self.w1_raw = put(f"{n}_w1_raw", [P, 2, DK, P], F32, at=at)
                self.w1_hi = put(f"{n}_w1_hi", [P, 2, DK, P], F32R)
                self.w1_lo = put(f"{n}_w1_lo", [P, 2, DK, P], F32R)
                self.w2_raw = put(f"{n}_w2_raw", [P, D], F32)
                self.u_f = put(f"{n}_u_f", [P, self.tok], F32)
                self.kept = plan["at"]
                self.w2_hi = put(f"{n}_w2_hi", [P, 2, D], F32R)
                self.w2_lo = put(f"{n}_w2_lo", [P, 2, D], F32R)
                self.u_hi = put(f"{n}_u_hi", [P, 3, self.tok], F32R)
                self.u_lo = put(f"{n}_u_lo", [P, 3, self.tok], F32R)

        room1 = Room()
        room1.tok = TOK
        room1.res = put("r1_res", [P, DK, TOK], F32, at=arena)
        room1.stream("r1", plan["at"])
        scratch = plan["at"]
        room1.hidden("r1", scratch)
        room1.norm("r1", scratch)
        assert plan["at"] <= room1.kept

        wp_raw = put("wp_raw", [P, 2, DK, P], F32, at=room1.kept)
        wp_hi = put("wp_hi", [P, 2, DK, P], F32R)
        wp_lo = put("wp_lo", [P, 2, DK, P], F32R)
        proj_c = put("proj_c", [P, 8, TOK], F32, at=arena)
        free1 = plan["at"]
        proj_l = put("proj_l", [P, 8, LAT], F32, at=free1 + 2 * DK * TOK * 4)
        free2 = plan["at"]
        kv_p, side_p, gk_p, gv_p = proj_c[:, 0], proj_c[:, 1], proj_c[:, 2:4], proj_c[:, 4:8]
        qa_p, gq_p, gg_p = proj_l[:, 0:2], proj_l[:, 2:4], proj_l[:, 4:8]

        cum = put("cum", [P, 4, TOK], F32, at=free1)
        v_tok = put("v_tok", [P, NC, GH, GDV], F32)
        state = put("state", [P, 4, NC, GDV], F32)
        attn = put("attn", [P, GH, NC_LAT, C], F32)
        decay = put("decay", [P, 4, NC], F32)
        assert plan["at"] <= free1 + 2 * DK * TOK * 4
        keep = put("keep", [P, TOK + 1], F32, at=free2)
        share = plan["at"]
        z = put("z", [P, 2, TOK], F32)
        zl = put("zl", [P, 2, TOK], F32)
        kd = put("kd", [P, 2, TOK], F32, at=share)
        kd_tok = put("kd_tok", [P, 2, NC, C], F32)
        diff = put("diff", [P, 2, 2, LAT], F32, at=share)
        q_lev = put("q_lev", [P, 2, LAT], F32)
        k_lev = put("k_lev", [P, 2, LAT], F32)
        q_dec = put("q_dec", [P, 4, LAT], F32, at=share)
        o_gla = put("o_gla", [P, GH, LAT], F32)
        g_sq = put("g_sq", [P, 2, BANK], F32)
        g_rstd = put("g_rstd", [P, 2, BANK], F32)
        mix_hi = put("mix_hi", [P, DK, LAT], F32R, at=arena + 2 * TOK * 4)
        mix_lo = put("mix_lo", [P, DK, LAT], F32R)
        after_mix = plan["at"]

        kvn_hi = put("kvn_hi", [P, TOK], F32R)
        kvn_lo = put("kvn_lo", [P, TOK], F32R)
        qn_hi = put("qn_hi", [P, 2, LAT], F32R)
        qn_lo = put("qn_lo", [P, 2, LAT], F32R)
        k_hi = put("k_hi", [P, 2, TOK], F32R)
        k_lo = put("k_lo", [P, 2, TOK], F32R)
        assert plan["at"] <= free1 + 2 * DK * TOK * 4
        q_f = put("q_f", [P, LAT], F32)
        q_hi = put("q_hi", [P, 2, LAT], F32R)
        q_lo = put("q_lo", [P, 2, LAT], F32R)
        v_at = plan["at"]
        v_hi = put("v_hi", [P, 2, NC, P], F32R)
        v_lo = put("v_lo", [P, 2, NC, P], F32R)
        p_at = plan["at"]
        p_f = put("p_f", [P, 4, BANK], F32)
        p_hi = put("p_hi", [P, 4, BANK], F32R)
        p_lo = put("p_lo", [P, 4, BANK], F32R)
        wq_raw = put("wq_raw", [P, 2, 2, P], F32)
        wq_hi = put("wq_hi", [P, 2, 2, P], F32R)
        wq_lo = put("wq_lo", [P, 2, 2, P], F32R)
        wkv_raw = put("wkv_raw", [P, 2, P], F32)
        wkv_hi = put("wkv_hi", [P, 2, P], F32R)
        wkv_lo = put("wkv_lo", [P, 2, P], F32R)
        rope = put("rope", [P, LAT], F32)
        pr_sq = put("pr_sq", [P, 2, LAT], F32, at=v_at)
        pr_r = put("pr_r", [P, TOK], F32)
        k_f = put("k_f", [P, TOK], F32)
        assert plan["at"] <= p_at
        k_rot = put("k_rot", [P, LAT], F32, at=p_at)
        acc_f = put("acc_f", [P, BANK], F32, at=arena)
        acc_r = put("acc_r", [P, BANK], F32)
        row_max = put("row_max", [P, LAT // P, QK + 1], F32)
        assert plan["at"] <= arena + 2 * TOK * 4

        room2 = Room()
        room2.tok = LAT
        room2.hidden("r2", arena)
        assert plan["at"] <= after_mix
        room2.stream("r2", plan["at"])
        assert plan["at"] >= after_mix
        room2_res = plan["at"]
        room2.res = put("r2_res", [P, DK, LAT], F32)
        room2.norm("r2", plan["at"], rstd=room2.u_f[:, :].rearrange("p (a b) -> p a b", b=BANK))
        wo_raw = put("wo_raw", [P, 2, DK, P], F32, at=after_mix)
        wo_hi = put("wo_hi", [P, 2, DK, P], F32R)
        wo_lo = put("wo_lo", [P, 2, DK, P], F32R)
        ada_c = Ada("ada_c", 5 * DK, 4 * DK, 1, ada_b.after, plan["at"])
        assert plan["at"] <= room2_res

        link_sem = {n: sem(f"{n}_link") for n in ("dve", "act", "pool")}
        count = {n: 0 for n in link_sem}

        def link(eng, name, ins):
            count[name] += 1
            ins.then_inc(link_sem[name], 1)
            eng.wait_ge(link_sem[name], count[name])

        consts_in = sem("consts_in")
        CONSTS = 16 * 9
        filled = sem("filled")
        CONST_FILLS, SCAN_FILLS, MLA_FILLS = 3, 5, 13
        ada_in = [sem(f"ada_in{i}") for i in range(4)]
        cond_in = sem("cond_in")
        cond_silu = sem("cond_silu")
        ada_mul = sem("ada_mul")
        gains_done = sem("gains_done")

        EXP_LN = "natural_log_exp_and_others"

        class Norms:
            def __init__(self, n, room, chunks, steps, post_s, pre_s, source, target):
                self.room, self.chunks, self.steps = room, chunks, steps
                self.post_s, self.pre_s, self.source, self.target = post_s, pre_s, source, target
                if self.posts():
                    self.x_in = sem(f"{n}_x_in")
                    self.added = sem(f"{n}_added")
                    self.stored = sem(f"{n}_stored")
                else:
                    self.x_in = [sem(f"{n}_x_in{c}") for c in range(len(chunks))]
                if len(steps) > len(self.posts()):
                    self.hi = sem(f"{n}_hi")
                    self.lo = sem(f"{n}_lo")
                self.squared = sem(f"{n}_squared")
                self.stat = sem(f"{n}_stat")
                self.rooted = sem(f"{n}_rooted")
                self.scaled = sem(f"{n}_scaled")

            def posts(self):
                return [c for kind, c in self.steps if kind == "post"]

        PARTS = (ada_a, ada_b, ada_c)

        def ada_cond(sp, a):
            sp.dma_start(a.cond[:, 0:a.conds], cond[0:a.conds].partition_broadcast(P)).then_inc(cond_in, 16)

        def ada_load(sp, a, t, slot):
            if not isinstance(t, int) or t >= 4:
                sp.wait_ge(ada_mul, t * a.conds + (a.before - 3 * a.conds))
            sp.dma_start(a.w[:, slot], w_ada[bass.ds(t + a.first, 1)].rearrange("a p k -> p (a k)"))\
                .then_inc(ada_in[slot], 16)

        def ada_silu(act, a):
            m = PARTS.index(a)
            act.wait_ge(cond_in, 16 * (m + 1))
            act.activation(a.cond[:, 0:a.conds], a.cond[:, 0:a.conds], ACT.Silu).then_inc(cond_silu, 1)

        def ada_tile(dve, a, t):
            if t == 0:
                dve.wait_ge(cond_silu, PARTS.index(a) + 1)
            dve.wait_ge(ada_in[t % 4], 16 * ((a.first + t) // 4 + 1))
            m, k = divmod(a.first + t, DK)
            for c in range(a.conds):
                n = a.before + t * a.conds + c
                if n >= 2:
                    dve.wait_ge(ada_mul, n - 1)
                dve.tensor_tensor_reduce(out=a.junk[:, n % 2], in0=a.w[:, t % 4], in1=a.cond[:, c], scale=1.0,
                                         scalar=0.0, op0=ALU.mult, op1=ALU.add,
                                         accum_out=mods[:, m, k, c:c + 1]).then_inc(ada_mul, 1)

        def ada_finish(dve, a, pre, post):
            m0, m1, w = a.first // DK, (a.first + a.tiles) // DK, slice(0, a.conds)
            dve.wait_ge(ada_mul, a.after)
            link(dve, "dve", dve.tensor_tensor(mods[:, m0:m1, :, w], mods[:, m0:m1, :, w], bada_sb[:, m0:m1, :, w],
                                               ALU.add))
            for s in pre:
                last = dve.scalar_tensor_tensor(out=gain_pre[:, s, :, w], in0=mods[:, 3 * s + 1, :, w], scalar=1.0,
                                                in1=pre_sb[:, s, :, w], op0=ALU.add, op1=ALU.mult)
            for s in post:
                last = dve.scalar_tensor_tensor(out=gain_post[:, s, :, w], in0=mods[:, 3 * s + 2, :, w],
                                                scalar=1.0 if s == 1 else 0.5, in1=post_sb[:, s, :, w],
                                                op0=ALU.mult, op1=ALU.mult)
            last.then_inc(gains_done, 1)
            dve.wait_ge(gains_done, PARTS.index(a) + 1)

        def norm_sync(sp, q, ready=None):
            posts = q.posts()
            if not posts:
                for c, (t0, w, _) in enumerate(q.chunks):
                    sp.dma_start(q.room.res[:, :, t0:t0 + w], q.source[:, :, t0:t0 + w]).then_inc(q.x_in[c], 16)
                return
            ready()

            def store(m):
                t0, w, _ = q.chunks[posts[m]]
                sp.wait_ge(q.added, (m + 1) * DK)
                sp.dma_start(q.target[:, :, t0:t0 + w], q.room.res[:, :, t0:t0 + w]).then_inc(q.stored, 16)

            for m, c in enumerate(posts):
                t0, w, _ = q.chunks[c]
                if m:
                    sp.wait_ge(q.added, m * DK)
                sp.dma_start(q.room.xin[:, :, 0:w], q.source[:, :, t0:t0 + w]).then_inc(q.x_in, 16)
                if m:
                    store(m - 1)
            store(len(posts) - 1)

        def norm_tensor(pe, q, bank_free=None):
            if bank_free:
                bank_free()
            for n, (_, c) in enumerate(q.steps):
                w = q.chunks[c][1]
                for k in range(DK):
                    pe.wait_ge(q.squared, n * DK + k + 1)
                    if n >= 2 and k == 0:
                        pe.wait_ge(q.rooted, n - 1)
                    pe.matmul(bank[:, 6 + n % 2, 0:w], ones[:, :], q.room.sq[:, k % 4, 0:w], start=(k == 0),
                              stop=(k == DK - 1)).then_inc(q.stat, 1)

        def norm_scalar(act, q, y_ready=None):
            act.preload_act_table_set(EXP_LN)
            room, pres = q.room, 0

            def highs(c, p):
                act.wait_ge(gains_done, q.pre_s + 1)
                t0, w, which = q.chunks[c]
                for k in range(DK):
                    act.wait_ge(q.scaled, q.steps.index(("pre", c)) * DK + k + 1)
                    act.activation(room.a_hi[:, k, t0:t0 + w], room.tmp[:, k % 2, 0:w], ACT.Identity,
                                   bias=mods[:, 3 * q.pre_s, k, which:which + 1]).then_inc(q.hi, 1)

            for n, (kind, c) in enumerate(q.steps):
                t0, w, which = q.chunks[c]
                for k in range(DK):
                    if kind == "post":
                        y_ready(c, k)
                    elif q.posts():
                        act.wait_ge(q.added, q.posts().index(c) * DK + k + 1)
                    else:
                        act.wait_ge(q.x_in[c], 16)
                    if n * DK + k >= 4:
                        act.wait_ge(q.stat, n * DK + k - 3)
                    act.activation(room.sq[:, k % 4, 0:w], room.res[:, k, t0:t0 + w], ACT.Square)\
                        .then_inc(q.squared, 1)
                act.wait_ge(q.stat, (n + 1) * DK)
                if n >= 2:
                    act.wait_ge(q.scaled, (n - 1) * DK)
                r = room.rstd[:, n % 2, 0:w]
                link(act, "act", act.activation(r, bank[:, 6 + n % 2, 0:w], ACT.Ln, bias=eps[:, :], scale=1.0 / D))
                act.activation(r, r, ACT.Exp, scale=-0.5).then_inc(q.rooted, 1)
                if kind == "pre":
                    highs(c, pres)
                    pres += 1

        def norm_vector(dve, q, a_free=None):
            room, pres = q.room, 0
            for n, (kind, c) in enumerate(q.steps):
                t0, w, which = q.chunks[c]
                dve.wait_ge(q.rooted, n + 1)
                gain = gain_post[:, q.post_s] if kind == "post" else gain_pre[:, q.pre_s]

                def low(k):
                    dve.wait_ge(q.hi, pres * DK + k + 1)
                    dve.scalar_tensor_tensor(out=room.a_lo[:, k, t0:t0 + w], in0=room.tmp[:, k % 2, 0:w],
                                             scalar=mods[:, 3 * q.pre_s, k, which:which + 1],
                                             in1=room.a_hi[:, k, t0:t0 + w].bitcast(F32), op0=ALU.add,
                                             op1=ALU.subtract).then_inc(q.lo, 1)

                for k in range(DK):
                    y = room.res[:, k, t0:t0 + w]
                    if kind == "pre" and k >= 2:
                        low(k - 2)
                        dve.wait_ge(q.lo, pres * DK + k - 1)
                    elif kind == "pre" and pres:
                        dve.wait_ge(q.lo, pres * DK)
                    dve.scalar_tensor_tensor(out=y if kind == "post" else room.tmp[:, k % 2, 0:w], in0=y,
                                             scalar=gain[:, k, which:which + 1], in1=room.rstd[:, n % 2, 0:w],
                                             op0=ALU.mult, op1=ALU.mult).then_inc(q.scaled, 1)
                if kind == "pre":
                    low(DK - 2)
                    low(DK - 1)
                    pres += 1

        def norm_pool(pool, q):
            for m, c in enumerate(q.posts()):
                t0, w, _ = q.chunks[c]
                n = q.steps.index(("post", c))
                pool.wait_ge(q.x_in, 16 * (m + 1))
                for k in range(DK):
                    pool.wait_ge(q.scaled, n * DK + k + 1)
                    y = q.room.res[:, k, t0:t0 + w]
                    pool.tensor_tensor(y, y, q.room.xin[:, k, 0:w], ALU.add).then_inc(q.added, 1)

        class Ffn:
            def __init__(self, n, s, room, chunks, norms):
                self.s, self.room, self.chunks, self.norms = s, room, chunks, norms
                self.tok = sum(w for _, w, _ in chunks)
                self.w_in, self.w_out = (f1_in, f1_out) if s == 0 else (f2_in, f2_out)
                self.w1_in = [sem(f"{n}_w1_in{i}") for i in range(2)]
                self.w2_in = sem(f"{n}_w2_in")
                self.w1_hi = sem(f"{n}_w1_hi")
                self.w1_lo = sem(f"{n}_w1_lo")
                self.w2_hi = sem(f"{n}_w2_hi")
                self.w2_lo = sem(f"{n}_w2_lo")
                self.half = sem(f"{n}_half")
                self.silu = sem(f"{n}_silu")
                self.u = sem(f"{n}_u")
                self.u_hi = sem(f"{n}_u_hi")
                self.u_lo = sem(f"{n}_u_lo")
                self.y_mm = sem(f"{n}_y_mm")
                self.y_add = sem(f"{n}_y_add")

        BOTH = [("post", 0), ("post", 1), ("pre", 0), ("post", 2), ("pre", 1), ("pre", 2)]
        n1 = Norms("n1", room1, CHUNKS, [("pre", 0), ("pre", 1), ("pre", 2)], None, 0, x_t, None)
        f1 = Ffn("f1", 0, room1, CHUNKS, n1)
        n2 = Norms("n2", room1, CHUNKS, BOTH, 0, 1, x_t, x1_d)

        n3 = Norms("n3", room2, CHUNKS[:2], [("post", 0), ("post", 1), ("pre", 0), ("pre", 1)], 1, 2, x1_d, x2_d)
        f2 = Ffn("f2", 2, room2, CHUNKS[:2], n3)
        n4 = Norms("n4", room2, CHUNKS[:2], [("post", 0), ("post", 1)], 2, None, x2_d, out)
        w_in_sem = [sem(f"w_in{i}") for i in range(2)]
        pj_hi, pj_lo, pj_mm, pj_out = (sem(f"pj_{n}") for n in ("hi", "lo", "mm", "out"))
        g_silu = sem("g_silu")
        z_mm, z_in, z_sp, z_cum = (sem(f"z_{n}") for n in ("mm", "in", "sp", "cum"))
        vt_mm, vt_out = sem("vt_mm"), sem("vt_out")
        kd_dif, kd_exp, kd_mul, kt_mm, kt_out, kv_mm, kv_add = (
            sem(f"g_{n}") for n in ("kd_dif", "kd_exp", "kd_mul", "kt_mm", "kt_out", "kv_mm", "kv_add"))
        lv_dif, lv_exp, lv_mul, lv_mm, lv_put, lv_base = (
            sem(f"lv_{n}") for n in ("dif", "exp", "mul", "mm", "put", "base"))
        qd_exp, qd_mul, o_mm, o_sq, o_out, o_stat, o_root, o_norm, o_hi, o_lo = (
            sem(f"go_{n}") for n in ("qd_exp", "qd_mul", "mm", "sq", "out", "stat", "root", "norm", "hi", "lo"))

        m_rope = sem("m_rope")
        m_w_in = [sem(f"m_w_in{i}") for i in range(2)]
        pr_sqd, pr_mm, pr_root, pr_mul, pr_hi, pr_lo, pr_rot, pr_khi, pr_klo = (
            sem(f"pr_{n}") for n in ("sqd", "mm", "root", "mul", "hi", "lo", "rot", "khi", "klo"))
        m_w_hi, m_w_lo, mk_mm, mk_hi, mk_lo, mq_mm, mq_raw, mq_rope, mq_hi, mq_lo, mv_mm, mv_hi, mv_lo = (
            sem(f"m_{n}") for n in ("w_hi", "w_lo", "k_mm", "k_hi", "k_lo", "q_mm", "q_raw", "q_rope", "q_hi", "q_lo",
                                    "v_mm", "v_hi", "v_lo"))
        c_mm, c_max, x_mm, x_row, s_mm, s_exp, pv_mm = (
            sem(f"m_{n}") for n in ("c_mm", "c_max", "x_mm", "x_row", "s_mm", "s_exp", "pv_mm"))
        part_hi = {"act": sem("m_p_hi_act"), "dve": sem("m_p_hi_dve")}
        part_lo = {"dve": sem("m_p_lo_dve"), "pool": sem("m_p_lo_pool")}
        acc_out, acc_root, acc_div, acc_hi, acc_lo = (sem(f"m_acc_{n}") for n in ("out", "root", "div", "hi", "lo"))
        wo_split_hi, wo_split_lo, wo_mm, wo_out = (sem(f"wo_{n}") for n in ("hi", "lo", "mm", "out"))

        block = ctx.enter_context(nc.Block())

        def over_tiles(eng, tile):
            tile(0, 0, 0)
            tile(1, 1, 0)
            with eng.Fori(0, 3) as i:
                for slot in range(2):
                    tile(i * 2 + (2 + slot), slot, 0)
            with eng.Fori(0, 4) as i:
                for slot in range(2):
                    tile(i * 2 + (8 + slot), slot, 1)

        def proj_sync(sp):
            def load(t, slot, group):
                if not isinstance(t, int):
                    sp.wait_ge(pj_lo, t - 1)
                sp.dma_start(wp_raw[:, slot], w_in[bass.ds(t, 1)].rearrange("a p k m -> p (a k) m"))\
                    .then_inc(w_in_sem[slot], 16)
            sp.wait_ge(f1.y_mm, PAIRS * DK * len(CHUNKS))
            over_tiles(sp, load)

        def proj_scalar(act):
            def split(t, slot, group):
                act.wait_ge(w_in_sem[slot], t * 8 + (16 - 8 * slot))
                if not isinstance(t, int) or t >= 2:
                    act.wait_ge(pj_mm, t - 1)
                act.activation(wp_hi[:, slot], wp_raw[:, slot], ACT.Copy).then_inc(pj_hi, 1)

            def leave(t, slot, group):
                tok = (TOK, LAT)[group]
                act.wait_ge(pj_mm, t + 1)
                src = bank[:, 3 * slot:3 * slot + 3].rearrange("p a b -> p (a b)")[:, 0:tok]
                dst = (proj_c, proj_l)[group][:, bass.ds(t - 8 * group, 1)].rearrange("p a b -> p (a b)")
                act.activation(dst, src, ACT.Copy).then_inc(pj_out, 1)

            split(0, 0, 0)
            split(1, 1, 0)
            act.wait_ge(n2.stored, 16 * len(CHUNKS))
            with act.Fori(0, 3) as i:
                for slot in range(2):
                    leave(i * 2 + slot, slot, 0)
                    split(i * 2 + (2 + slot), slot, 0)
            for slot in range(2):
                leave(6 + slot, slot, 0)
                split(8 + slot, slot, 1)
            with act.Fori(0, 3) as i:
                for slot in range(2):
                    leave(i * 2 + (8 + slot), slot, 1)
                    split(i * 2 + (10 + slot), slot, 1)
            leave(14, 0, 1)
            leave(15, 1, 1)

        def proj_vector(dve):
            def split(t, slot, group):
                dve.wait_ge(pj_hi, t + 1)
                dve.tensor_tensor(wp_lo[:, slot], wp_raw[:, slot], wp_hi[:, slot].bitcast(F32),
                                  ALU.subtract).then_inc(pj_lo, 1)
            over_tiles(dve, split)

        def proj_tensor(pe):
            def tile(t, slot, group):
                pe.wait_ge(pj_lo, t + 1)
                if not isinstance(t, int):
                    pe.wait_ge(pj_out, t - 1)
                for c, (t0, w, _) in enumerate(CHUNKS[:3 - group]):
                    pe.wait_ge(n2.lo, DK * (c + 1))
                    acc = bank[:, 3 * slot + c, 0:w]
                    for k in range(DK):
                        hi, lo = room1.a_hi[:, k, t0:t0 + w], room1.a_lo[:, k, t0:t0 + w]
                        pe.matmul(acc, wp_hi[:, slot, k], hi, start=(k == 0), stop=False)
                        pe.matmul(acc, wp_hi[:, slot, k], lo, start=False, stop=False)
                        last = pe.matmul(acc, wp_lo[:, slot, k], hi, start=False, stop=(k == DK - 1))
                last.then_inc(pj_mm, 1)
            over_tiles(pe, tile)

        def halves(ap, s):
            return ap.rearrange("p (b h s) -> p b h s", h=2, s=s)

        def edge(ap, s, right):
            h = halves(ap, s)
            e = h[:, :, 1, 0:1] if right else h[:, :, 0, s - 1:s]
            return e.to_broadcast([P, LAT // (2 * s), s])

        LAST = (C - 1, 0)
        ORDER = ([8, 9] + list(range(8)), [9, 8] + list(range(7, -1, -1)))

        def gla_tensor(pe):
            pe.wait_ge(consts_in, CONSTS)
            pe.wait_ge(pj_out, 16)
            for i in range(4):
                if i >= 2:
                    pe.wait_ge(z_in, i - 1)
                for c, (t0, w, _) in enumerate(CHUNKS):
                    last = pe.matmul(bank[:, 3 * (i % 2) + c, 0:w], wa_sb[0:2 * GRANK, i],
                                     side_p[0:2 * GRANK, t0:t0 + w], start=True, stop=True)
                last.then_inc(z_mm, 1)
            for c in range(NC):
                if c >= 2:
                    pe.wait_ge(vt_out, c - 1)
                for h in range(GH):
                    last = pe.transpose(bank[:, 6 + c % 2, h * P:(h + 1) * P], gv_p[:, h, c * C:(c + 1) * C],
                                        ident[:, :])
                last.then_inc(vt_mm, 1)
            pe.wait_ge(z_in, 4)
            pe.wait_ge(vt_out, NC)
            for i in range(4):
                d, p = divmod(i, 2)
                pe.wait_ge(kd_mul, i + 1)
                if i:
                    pe.wait_ge(kt_out, i)
                for c in range(NC):
                    last = pe.transpose(bank[:, c // 4, c % 4 * C:(c % 4 + 1) * C],
                                        kd[:, i % 2, c * C:(c + 1) * C], ident[:, :])
                last.then_inc(kt_mm, 1)
                pe.wait_ge(kt_out, i + 1)
                if i:
                    pe.wait_ge(kv_add, 9 * i)
                for n, c in enumerate(ORDER[d][:-1]):
                    pe.matmul(bank[:, 3 + n // 2, n % 2 * 2 * GDV:(n % 2 + 1) * 2 * GDV], kd_tok[:, i % 2, c],
                              v_tok[:, c, 2 * p:2 * p + 2].rearrange("p a b -> p (a b)"), start=True,
                              stop=True).then_inc(kv_mm, 1)
            pe.wait_ge(kt_out, 4)
            pe.wait_ge(kv_add, 36)
            for n in range(2 * (LEVELS + 1)):
                level, p = divmod(n, 2)
                pe.wait_ge(lv_mul, n + 1)
                if n >= 2:
                    if n < 4:
                        pe.wait_ge(lv_base, n - 1)
                    else:
                        pe.wait_ge(lv_put, n - 3)
                k_of = gk_p[:, p] if level == LEVELS else k_lev[:, n % 2]
                for hh in range(2):
                    rows = slice(64 * hh, 64 * hh + 64)
                    for c in range(NC_LAT):
                        last = pe.matmul(bank[:, 4 * (n % 2) + 2 * hh + c // 4, c % 4 * C:(c % 4 + 1) * C],
                                         k_of[rows, c * C:(c + 1) * C], q_lev[rows, n % 2, c * C:(c + 1) * C],
                                         start=True, stop=True)
                last.then_inc(lv_mm, 1)
            pe.wait_ge(lv_put, 2 * LEVELS)
            pe.wait_ge(qd_mul, 4)
            for n in range(2 * GH):
                h, quad = divmod(n, 2)
                p, rows = h // 2, slice(64 * (h % 2), 64 * (h % 2) + 64)
                for c in range(4 * quad, 4 * quad + 4):
                    acc = bank[:, n, c % 4 * C:(c % 4 + 1) * C]
                    pe.matmul(acc, v_tok[:, c, h], attn[:, h, c], start=True, stop=False)
                    for d in range(2):
                        last = pe.matmul(acc, state[rows, 2 * d + p, c], q_dec[rows, 2 * d + p, c * C:(c + 1) * C],
                                         start=False, stop=(d == 1))
                last.then_inc(o_mm, 1)
            for n in range(2 * GH):
                pe.wait_ge(o_out, n + 1)
                pe.matmul(bank[:, n], ones[:, :], g_sq[:, n % 2], start=True, stop=True).then_inc(o_stat, 1)

        def gla_scalar(act):
            act.wait_ge(pj_out, 16)
            act.activation(gg_p.rearrange("p a b -> p (a b)"), gg_p.rearrange("p a b -> p (a b)"), ACT.Silu)\
                .then_inc(g_silu, 1)
            act.preload_act_table_set(EXP_LN)
            for i in range(4):
                act.wait_ge(z_in, i + 1)
                t = zl[:, i % 2]
                link(act, "act", act.activation(t, z[:, i % 2], ACT.Abs))
                link(act, "act", act.activation(t, t, ACT.Exp, scale=-1.0))
                act.activation(t, t, ACT.Ln, bias=1.0).then_inc(z_sp, 1)
            for c in range(NC):
                act.wait_ge(vt_mm, c + 1)
                act.activation(v_tok[:, c].rearrange("p a b -> p (a b)"), bank[:, 6 + c % 2], ACT.Copy)\
                    .then_inc(vt_out, 1)
            for i in range(4):
                d = i // 2
                act.wait_ge(kd_dif, i + 1)
                act.activation(kd[:, i % 2], kd[:, i % 2], ACT.Exp, scale=1 / GATE_NORM).then_inc(kd_exp, 1)
                last = cum[:, i].rearrange("p (c t) -> p c t", t=C)[:, :, LAST[d]]
                act.activation(decay[:, i], last, ACT.Exp, scale=1 / GATE_NORM).then_inc(kd_exp, 1)
                act.wait_ge(kt_mm, i + 1)
                src = bank[:, 0:3].rearrange("p a b -> p (a b)")[:, 0:TOK]
                if i >= 2:
                    act.wait_ge(kv_mm, 9 * (i - 1))
                act.activation(kd_tok[:, i % 2].rearrange("p a b -> p (a b)"), src, ACT.Copy).then_inc(kt_out, 1)
            for n in range(2 * LEVELS):
                act.wait_ge(lv_dif, n + 1)
                t = diff[:, n % 2].rearrange("p a b -> p (a b)")
                act.activation(t, t, ACT.Exp, scale=1 / GATE_NORM).then_inc(lv_exp, 1)
                if n in (2, 3):
                    act.wait_ge(lv_mm, n - 1)
                    act.activation(attn[:, 2 * (n - 2):2 * (n - 2) + 2].rearrange("p a b c -> p (a b c)"),
                                   bank[:, 4 * (n - 2):4 * (n - 2) + 4].rearrange("p a b -> p (a b)"), ACT.Copy)\
                        .then_inc(lv_base, 1)
            act.wait_ge(lv_mm, 2 * (LEVELS + 1))
            for i in range(4):
                act.activation(q_dec[:, i], cum[:, i, 0:LAT], ACT.Exp, scale=1 / GATE_NORM).then_inc(qd_exp, 1)
            for n in range(2 * GH):
                h, quad = divmod(n, 2)
                act.wait_ge(o_mm, n + 1)
                if n >= 2:
                    act.wait_ge(o_stat, n - 1)
                act.activation(g_sq[:, n % 2], bank[:, n], ACT.Square, scale=GDK ** -0.5).then_inc(o_sq, 1)
                act.activation(o_gla[:, h, quad * BANK:(quad + 1) * BANK], bank[:, n], ACT.Copy,
                               scale=GDK ** -0.5).then_inc(o_out, 1)
                if n:
                    root(act, n - 1)
            root(act, 2 * GH - 1)
            for n in range(2 * GH):
                h, quad = divmod(n, 2)
                act.wait_ge(o_norm, n + 1)
                t0 = quad * BANK
                act.activation(mix_hi[:, GH + h, t0:t0 + BANK], o_gla[:, h, t0:t0 + BANK], ACT.Copy)\
                    .then_inc(o_hi, 1)

        def root(act, n):
            act.wait_ge(o_stat, n + 1)
            if n >= 2:
                act.wait_ge(o_norm, n - 1)
            r = g_rstd[:, n % 2]
            link(act, "act", act.activation(r, bank[:, n], ACT.Ln, bias=eps[:, :], scale=1.0 / GDV))
            act.activation(r, r, ACT.Exp, scale=-0.5).then_inc(o_root, 1)

        def gla_vector(dve):
            dve.wait_ge(filled, SCAN_FILLS)
            for i in range(4):
                dve.wait_ge(z_mm, i + 1)
                if i >= 2:
                    dve.wait_ge(z_cum, 2 * (i - 1))
                src = bank[:, 3 * (i % 2):3 * (i % 2) + 3].rearrange("p a b -> p (a b)")[:, 0:TOK]
                dve.tensor_scalar(z[:, i % 2], src, ba_sb[:, i:i + 1], None, ALU.add).then_inc(z_in, 1)
                if i:
                    gla_sum(dve, i - 1)
            gla_sum(dve, 3)
            dve.wait_ge(z_cum, 8)
            dve.wait_ge(z_sp, 4)
            for i in range(4):
                d, p = divmod(i, 2)
                v = cum[:, i].rearrange("p (c t) -> p c t", t=C)
                if i >= 2:
                    dve.wait_ge(kt_mm, i - 1)
                t = kd[:, i % 2].rearrange("p (c t) -> p c t", t=C)
                dve.tensor_tensor(t, v[:, :, LAST[d]:LAST[d] + 1].to_broadcast([P, NC, C]), v, ALU.subtract)\
                    .then_inc(kd_dif, 1)
                dve.wait_ge(kd_exp, 2 * i + 2)
                dve.tensor_tensor(kd[:, i % 2], kd[:, i % 2], gk_p[:, p], ALU.mult).then_inc(kd_mul, 1)
                if i:
                    gla_chain(dve, i - 1)
            gla_chain(dve, 3)
            for n in range(2 * (LEVELS + 1)):
                level, p = divmod(n, 2)
                s = C // 2 >> level
                if n >= 2:
                    dve.wait_ge(lv_mul, n - 1)
                else:
                    dve.wait_ge(kt_mm, 4)
                    dve.wait_ge(kv_mm, 36)
                if level < LEVELS:
                    for d in range(2):
                        v, t = halves(cum[:, 2 * d + p, 0:LAT], s), halves(diff[:, n % 2, d], s)
                        e = edge(cum[:, 2 * d + p, 0:LAT], s, right=bool(d))
                        far = 1 - d
                        dve.tensor_tensor(t[:, :, far], v[:, :, far], e, ALU.subtract)
                        last = dve.tensor_tensor(t[:, :, 1 - far], e, v[:, :, 1 - far], ALU.subtract)
                    last.then_inc(lv_dif, 1)
                else:
                    dve.wait_ge(lv_mul, n)
                    dve.wait_ge(lv_mm, n - 1)
                    dve.tensor_scalar(q_lev[:, n % 2], gq_p[:, p], 2.0, None, ALU.mult).then_inc(lv_mul, 1)
                if n >= 4:
                    gla_put(dve, n - 2)
            gla_put(dve, 2 * LEVELS)
            gla_put(dve, 2 * LEVELS + 1)
            for i in range(4):
                dve.wait_ge(qd_exp, i + 1)
                dve.tensor_tensor(q_dec[:, i], q_dec[:, i], gq_p[:, i % 2], ALU.mult).then_inc(qd_mul, 1)
            dve.wait_ge(g_silu, 1)
            for n in range(2 * GH):
                h, quad = divmod(n, 2)
                t0 = quad * BANK
                dve.wait_ge(o_root, n + 1)
                o = o_gla[:, h, t0:t0 + BANK]
                link(dve, "dve", dve.scalar_tensor_tensor(out=o, in0=o, scalar=gnorm_sb[:, 0:1], in1=g_rstd[:, n % 2],
                                                          op0=ALU.mult, op1=ALU.mult))
                dve.tensor_tensor(o, o, gg_p[:, h, t0:t0 + BANK], ALU.mult).then_inc(o_norm, 1)
            for n in range(2 * GH):
                gla_low(dve, n)

        def gla_low(dve, n):
            h, t0 = n // 2, n % 2 * BANK
            dve.wait_ge(o_mm, 2 * GH)
            dve.wait_ge(o_hi, n + 1)
            dve.tensor_tensor(mix_lo[:, GH + h, t0:t0 + BANK], o_gla[:, h, t0:t0 + BANK],
                              mix_hi[:, GH + h, t0:t0 + BANK].bitcast(F32), ALU.subtract).then_inc(o_lo, 1)

        def gla_sum(dve, i):
            dve.wait_ge(z_sp, i + 1)
            t = zl[:, i % 2]
            dve.scalar_tensor_tensor(out=t, in0=z[:, i % 2], scalar=0.0, in1=t, op0=ALU.min,
                                     op1=ALU.subtract).then_inc(z_cum, 1)
            dve.wait_ge(z_cum, 2 * i + 1)
            if i < 2:
                dve.tensor_tensor_scan(cum[:, i], keep[:, 0:TOK], t, 0.0, ALU.mult, ALU.add).then_inc(z_cum, 1)
            else:
                dve.tensor_tensor_scan(cum[:, i, ::-1], keep[:, 1:TOK + 1][:, ::-1], t[:, ::-1], 0.0, ALU.mult,
                                       ALU.add).then_inc(z_cum, 1)

        def gla_chain(dve, i):
            d = i // 2
            for n, c in enumerate(ORDER[d][:-1]):
                dve.wait_ge(kv_mm, 9 * i + min(NC - 1, n // 2 * 2 + 2))
                if n:
                    dve.wait_ge(kv_add, 9 * i + n)
                after = ORDER[d][n + 1]
                for hh in range(2):
                    rows = slice(64 * hh, 64 * hh + 64)
                    kv = bank[rows, 3 + n // 2, (n % 2 * 2 + hh) * GDV:(n % 2 * 2 + hh + 1) * GDV]
                    if n:
                        last = dve.scalar_tensor_tensor(out=state[rows, i, after], in0=state[rows, i, c],
                                                        scalar=decay[rows, i, c:c + 1], in1=kv, op0=ALU.mult,
                                                        op1=ALU.add)
                    else:
                        last = dve.tensor_copy(state[rows, i, after], kv)
                last.then_inc(kv_add, 1)

        def gla_put(dve, n):
            level, p = divmod(n, 2)
            dve.wait_ge(lv_mm, n + 1)
            dve.wait_ge(lv_base, 2)
            if n >= 4:
                dve.wait_ge(lv_put, n - 3)
            for hh in range(2):
                for quad in range(2):
                    last = dve.copy_predicated(attn[:, 2 * p + hh, 4 * quad:4 * quad + 4].rearrange("p a b -> p (a b)"),
                                               mask[:, level - 1], bank[:, 4 * (n % 2) + 2 * hh + quad])
            last.then_inc(lv_put, 1)

        def gla_pool(pool):
            pool.wait_ge(pj_mm, 16)
            pool.memset(keep[:, :], 1.0).then_inc(filled, 1)
            pool.wait_ge(filled, SCAN_FILLS - 1)
            for c in range(NC + 1):
                last = pool.memset(keep[:, c * C:c * C + 1], 0.0)
            last.then_inc(filled, 1)
            for n in range(2 * LEVELS):
                level, p = divmod(n, 2)
                s = C // 2 >> level
                pool.wait_ge(lv_exp, n + 1)
                if n >= 2:
                    pool.wait_ge(lv_mm, n - 1)
                f, b = halves(diff[:, n % 2, 0], s), halves(diff[:, n % 2, 1], s)
                q, k = halves(gq_p[:, p], s), halves(gk_p[:, p, 0:LAT], s)
                ql, kl = halves(q_lev[:, n % 2], s), halves(k_lev[:, n % 2], s)
                pool.tensor_tensor(ql[:, :, 1], q[:, :, 1], f[:, :, 1], ALU.mult)
                pool.tensor_tensor(ql[:, :, 0], q[:, :, 0], b[:, :, 0], ALU.mult)
                pool.tensor_tensor(kl[:, :, 0], k[:, :, 0], f[:, :, 0], ALU.mult)
                pool.tensor_tensor(kl[:, :, 1], k[:, :, 1], b[:, :, 1], ALU.mult).then_inc(lv_mul, 1)


        PAIRS = FJ // 2

        def over_hidden(eng, prologue, pair, tail):
            prologue()
            with eng.Fori(0, (PAIRS - 1) // 2) as i:
                for k in range(2):
                    pair(i * 2 + (k + 1), 2 if k == 0 else 0)
            tail()

        def ffn_sync(sp, f, more=lambda: None):
            def load_half(j, half):
                if not isinstance(j, int) or j >= 1:
                    sp.wait_ge(f.w1_lo, j * 2 + (half - 1))
                sp.dma_start(f.room.w1_raw[:, half], f.w_in[bass.ds(j * 2 + half, 1)].rearrange("a p k m -> p (a k) m"))\
                    .then_inc(f.w1_in[half], 16)

            def load_w2(j):
                if not isinstance(j, int) or j >= 1:
                    sp.wait_ge(f.w2_lo, j)
                sp.dma_start(f.room.w2_raw[:, :], f.w_out[bass.ds(j, 1)].rearrange("a p m -> p (a m)")).then_inc(f.w2_in, 16)

            def prologue():
                for j in range(2):
                    load_half(j, 0)
                    load_half(j, 1)
                load_w2(0)
                more()
                load_w2(1)

            def pair(g, even):
                for t in range(2):
                    load_half(g * 2 + t, 0)
                    load_half(g * 2 + t, 1)
                    load_w2(g * 2 + t)

            over_hidden(sp, prologue, pair, lambda: None)

        def ffn_tensor(pe, f):
            nch = len(f.chunks)

            def hidden(j):
                for half in range(2):
                    pe.wait_ge(f.w1_lo, j * 2 + (half + 1))
                    if not isinstance(j, int) or j >= 1:
                        pe.wait_ge(f.silu if half == 0 else f.u, j)
                    for c, (t0, w, _) in enumerate(f.chunks):
                        pe.wait_ge(f.norms.lo, DK * (c + 1))
                        acc = bank[:, 3 * half + c, 0:w]
                        for k in range(DK):
                            hi, lo = f.room.a_hi[:, k, t0:t0 + w], f.room.a_lo[:, k, t0:t0 + w]
                            pe.matmul(acc, f.room.w1_hi[:, half, k], hi, start=(k == 0), stop=False)
                            pe.matmul(acc, f.room.w1_hi[:, half, k], lo, start=False, stop=False)
                            last = pe.matmul(acc, f.room.w1_lo[:, half, k], hi, start=False, stop=(k == DK - 1))
                    last.then_inc(f.half, 1)

            def project(g, even):
                pe.wait_ge(f.u_lo, g * 2 + 2)
                pe.wait_ge(f.w2_lo, g * 2 + 2)
                for c, (t0, w, _) in enumerate(f.chunks):
                    for m in range(DK):
                        n = c * DK + m
                        pe.wait_ge(f.y_add, g * (DK * nch) + (n + 1))
                        acc = bank[:, 6 + n % 2, 0:w]
                        for i, slot in enumerate((even, 1)):
                            hi, lo = f.room.u_hi[:, slot, t0:t0 + w], f.room.u_lo[:, slot, t0:t0 + w]
                            w_hi, w_lo = f.room.w2_hi[:, i, m * P:(m + 1) * P], f.room.w2_lo[:, i, m * P:(m + 1) * P]
                            pe.matmul(acc, w_hi, hi, start=(i == 0), stop=False)
                            pe.matmul(acc, w_hi, lo, start=False, stop=False)
                            last = pe.matmul(acc, w_lo, hi, start=False, stop=(i == 1))
                        last.then_inc(f.y_mm, 1)

            def prologue():
                hidden(0)
                hidden(1)

            def pair(g, even):
                hidden(g * 2)
                project(g - 1, 2 - even)
                hidden(g * 2 + 1)

            over_hidden(pe, prologue, pair, lambda: project(PAIRS - 1, 0))

        def ffn_scalar(act, f, more=lambda: None):
            nch = len(f.chunks)

            def w1_high(j, half):
                act.wait_ge(f.w1_in[half], (j + 1) * 16)
                if not isinstance(j, int) or j >= 1:
                    act.wait_ge(f.half, j * 2 + (half - 1))
                act.activation(f.room.w1_hi[:, half], f.room.w1_raw[:, half], ACT.Copy).then_inc(f.w1_hi, 1)

            def w2_high(j, slot):
                act.wait_ge(f.w2_in, (j + 1) * 16)
                if not isinstance(j, int) or j >= 2:
                    act.wait_ge(f.y_mm, (j - slot) * (DK * nch // 2))
                act.activation(f.room.w2_hi[:, slot], f.room.w2_raw[:, :], ACT.Copy).then_inc(f.w2_hi, 1)

            def silu(j):
                act.wait_ge(f.half, j * 2 + 1)
                if not isinstance(j, int) or j >= 1:
                    act.wait_ge(f.u_lo, j)
                gate = bank[:, 0:3].rearrange("p a b -> p (a b)")[:, 0:f.tok]
                act.activation(f.room.u_f[:, 0:f.tok], gate, ACT.Silu).then_inc(f.silu, 1)

            def u_high(j, slot):
                act.wait_ge(f.u, j + 1)
                act.activation(f.room.u_hi[:, slot, 0:f.tok], f.room.u_f[:, 0:f.tok], ACT.Copy).then_inc(f.u_hi, 1)

            def prologue():
                w1_high(0, 0)
                w1_high(0, 1)
                more()
                w1_high(1, 0)
                silu(0)
                w1_high(1, 1)
                u_high(0, 0)
                w2_high(0, 0)
                w1_high(2, 0)
                silu(1)
                w1_high(2, 1)
                u_high(1, 1)
                w2_high(1, 1)

            def pair(g, even, last=False):
                w1_high(g * 2 + 1, 0)
                silu(g * 2)
                w1_high(g * 2 + 1, 1)
                u_high(g * 2, even)
                w2_high(g * 2, 0)
                if not last:
                    w1_high(g * 2 + 2, 0)
                silu(g * 2 + 1)
                if not last:
                    w1_high(g * 2 + 2, 1)
                u_high(g * 2 + 1, 1)
                w2_high(g * 2 + 1, 1)

            act.preload_act_table_set("silu_and_others")
            prologue()
            with act.Fori(0, (PAIRS - 3) // 2) as i:
                pair(i * 2 + 1, 2)
                pair(i * 2 + 2, 0)
            pair(PAIRS - 2, 2)
            pair(PAIRS - 1, 0, last=True)

        def ffn_vector(dve, f, more=lambda: None):
            nch = len(f.chunks)

            def w1_low(j, half):
                dve.wait_ge(f.w1_hi, j * 2 + (half + 1))
                dve.tensor_tensor(f.room.w1_lo[:, half], f.room.w1_raw[:, half], f.room.w1_hi[:, half].bitcast(F32),
                                  ALU.subtract).then_inc(f.w1_lo, 1)

            def w2_low(j, slot):
                dve.wait_ge(f.w2_hi, j + 1)
                dve.tensor_tensor(f.room.w2_lo[:, slot], f.room.w2_raw[:, :], f.room.w2_hi[:, slot].bitcast(F32),
                                  ALU.subtract).then_inc(f.w2_lo, 1)

            def gated(j):
                dve.wait_ge(f.half, j * 2 + 2)
                dve.wait_ge(f.silu, j + 1)
                value = bank[:, 3:6].rearrange("p a b -> p (a b)")[:, 0:f.tok]
                dve.tensor_tensor(f.room.u_f[:, 0:f.tok], f.room.u_f[:, 0:f.tok], value, ALU.mult).then_inc(f.u, 1)

            def u_low(j, slot):
                dve.wait_ge(f.u_hi, j + 1)
                dve.tensor_tensor(f.room.u_lo[:, slot, 0:f.tok], f.room.u_f[:, 0:f.tok], f.room.u_hi[:, slot, 0:f.tok].bitcast(F32),
                                  ALU.subtract).then_inc(f.u_lo, 1)

            def add(g, c, m):
                t0, w, _ = f.chunks[c]
                n = c * DK + m
                dve.wait_ge(f.y_mm, g * (DK * nch) + (n + 1))
                y = f.room.res[:, m, t0:t0 + w]
                dve.tensor_tensor(y, y, bank[:, 6 + n % 2, 0:w], ALU.add).then_inc(f.y_add, 1)

            def prologue():
                w1_low(0, 0)
                w1_low(0, 1)
                w1_low(1, 0)
                more()
                gated(0)
                w1_low(1, 1)
                more()
                u_low(0, 0)
                w2_low(0, 0)
                more()
                w1_low(2, 0)
                gated(1)
                w1_low(2, 1)
                u_low(1, 1)
                w2_low(1, 1)

            def pair(g, even, last=False):
                w1_low(g * 2 + 1, 0)
                for n in range(DK * nch):
                    add(g - 1, n // DK, n % DK)
                    if n == 3:
                        gated(g * 2)
                    if n == 6:
                        w1_low(g * 2 + 1, 1)
                    if n == 9:
                        u_low(g * 2, even)
                w2_low(g * 2, 0)
                if not last:
                    w1_low(g * 2 + 2, 0)
                gated(g * 2 + 1)
                if not last:
                    w1_low(g * 2 + 2, 1)
                u_low(g * 2 + 1, 1)
                w2_low(g * 2 + 1, 1)

            prologue()
            dve.wait_ge(f.y_add, 2)
            with dve.Fori(0, (PAIRS - 3) // 2) as i:
                pair(i * 2 + 1, 2)
                pair(i * 2 + 2, 0)
            pair(PAIRS - 2, 2)
            pair(PAIRS - 1, 0, last=True)
            for n in range(DK * nch):
                add(PAIRS - 1, n // DK, n % DK)

        SCALE = QK ** -0.5
        UNITS = 2 * NC
        QT = LAT // P
        AHEAD = 3
        TURN = 15
        HI_ON = ["act" if n % 2 == 0 else "dve" for n in range(UNITS)]
        LO_ON = ["dve" if n % 2 == 0 else "pool" for n in range(UNITS)]
        COARSE = dict(zip((6, 7, 8, 10, 11, 12, 13, 14), range(QT)))
        NUM = (slice(0, 64), slice(64, 128))
        DEN = (slice(64, 128), slice(0, 64))
        VCOL = (0, 64)

        def split_done(eng, sems, on, h, n):
            who = on[n]
            eng.wait_ge(sems[who], h * on.count(who) + on[:n + 1].count(who))

        def over_heads(eng, first, body):
            first()
            with eng.Fori(0, HEADS // 2 - 1) as i:
                for slot in range(2):
                    body(i * 2 + slot, slot, False)
            body(HEADS - 2, 0, False)
            body(HEADS - 1, 1, True)

        def after(h, slot, n):
            return (h, slot, n + AHEAD) if n + AHEAD < UNITS else (h + 1, 1 - slot, n + AHEAD - UNITS)

        def mla_sync(sp):
            sp.wait_ge(o_lo, 2 * GH)
            sp.dma_start(rope[:, :], rope_d).then_inc(m_rope, 16)

            def load(h, slot):
                sp.dma_start(wq_raw[:, slot], w_qb[bass.ds(h, 1)].rearrange("a p k m -> p (a k) m"))\
                    .then_inc(m_w_in[slot], 16)
                sp.dma_start(wkv_raw[:, slot], w_kvb[bass.ds(h, 1)].rearrange("a p m -> p (a m)"))\
                    .then_inc(m_w_in[slot], 16)

            load(0, 0)
            load(1, 1)
            with sp.Fori(0, HEADS // 2 - 1) as i:
                for slot in range(2):
                    h = i * 2 + slot
                    sp.wait_ge(m_w_lo, h * 2 + 2)
                    load(h + 2, slot)

        def mla_pool(pool):
            pool.wait_ge(o_lo, 2 * GH)
            pool.memset(k_hi[QK:QK + 1, :, :].bitcast(F32), 1.0).then_inc(filled, 1)
            pool.memset(k_lo[QK:QK + 1, :, :].bitcast(F32), 0.0).then_inc(filled, 1)
            pool.memset(q_lo[QK:QK + 1, :, :].bitcast(F32), 0.0).then_inc(filled, 1)
            pool.wait_ge(filled, SCAN_FILLS + 3)
            pool.wait_ge(pr_klo, 2)
            pool.memset(row_max[:, :, :], 0.0).then_inc(filled, 1)
            pool.memset(acc_f[:, :], 0.0).then_inc(acc_lo, 1)
            pool.memset(acc_r[:, :], 0.0).then_inc(acc_out, 1)
            for slot in range(2):
                cols = slice(64 - VCOL[slot], 128 - VCOL[slot])
                pool.memset(v_hi[:, slot, :, cols].bitcast(F32), 1.0).then_inc(filled, 1)
                pool.memset(v_lo[:, slot, :, cols].bitcast(F32), 0.0).then_inc(filled, 1)

            def first():
                for n in range(AHEAD):
                    low(pool, "pool", 0, n)

            def body(h, slot, last):
                for n in range(UNITS):
                    g, _, m = after(h, slot, n)
                    if not (last and n + AHEAD >= UNITS):
                        low(pool, "pool", g, m)

            over_heads(pool, first, body)

        def low(eng, who, h, n):
            if LO_ON[n] == who:
                split_done(eng, part_hi, HI_ON, h, n)
                eng.tensor_tensor(p_lo[:, n % 4], p_f[:, n % 4], p_hi[:, n % 4].bitcast(F32), ALU.subtract)\
                    .then_inc(part_lo[who], 1)

        def mla_tensor(pe):
            for k in range(3):
                pe.wait_ge(pr_sqd, 1)
                t0, w, _ = CHUNKS[k]
                last = pe.matmul(bank[:, k, 0:w], ones[:, :], pr_sq[:, :, :].rearrange("p a b -> p (a b)")[:, t0:t0 + w],
                                 start=True, stop=True)
            last.then_inc(pr_mm, 1)
            pe.wait_ge(pr_sqd, 2)
            for c in range(2):
                for k in range(2):
                    last = pe.matmul(bank[:, 3 + c], ones[:, :], pr_sq[:, k, c * BANK:(c + 1) * BANK], start=(k == 0),
                                     stop=(k == 1))
            last.then_inc(pr_mm, 1)
            pe.wait_ge(filled, MLA_FILLS)

            def three(acc, w_hi, w_lo, x_hi, x_lo, start=True, stop=True):
                pe.matmul(acc, w_hi, x_hi, start=start, stop=False)
                pe.matmul(acc, w_hi, x_lo, start=False, stop=False)
                return pe.matmul(acc, w_lo, x_hi, start=False, stop=stop)

            def keys(h, slot):
                pe.wait_ge(m_w_lo, h * 2 + 2)
                pe.wait_ge(x_row, h)
                for c, (t0, w, _) in enumerate(CHUNKS):
                    last = three(bank[:, c, 0:w], wkv_hi[:, slot], wkv_lo[:, slot], kvn_hi[:, t0:t0 + w],
                                 kvn_lo[:, t0:t0 + w])
                last.then_inc(mk_mm, 1)

            def queries(h, slot):
                pe.wait_ge(mk_lo, h + 1)
                for c in range(2):
                    for k in range(2):
                        x = slice(c * BANK, (c + 1) * BANK)
                        last = three(bank[:, c], wq_hi[:, slot, k], wq_lo[:, slot, k], qn_hi[:, k, x], qn_lo[:, k, x],
                                     k == 0, k == 1)
                last.then_inc(mq_mm, 1)

            def values(h, slot):
                pe.wait_ge(mq_rope, h * 3 + 3)
                pe.wait_ge(mq_raw, h + 1)
                acc = bank[:, 0:2].rearrange("p a b -> p (a b)")
                for t in range(NC):
                    x = slice(t * C, (t + 1) * C)
                    last = three(acc[:, t * VD:(t + 1) * VD], kvn_hi[:, x], kvn_lo[:, x], wkv_hi[:, slot, NOPE:],
                                 wkv_lo[:, slot, NOPE:])
                last.then_inc(mv_mm, 1)

            def coarse(h, slot, t):
                if t == 0:
                    pe.wait_ge(mq_hi, h + 1)
                    pe.wait_ge(mv_lo, h + 1)
                pe.wait_ge(c_max, h * QT + t)
                for c, (t0, w, _) in enumerate(CHUNKS):
                    last = pe.matmul(bank[:, c, 0:w], q_hi[0:QK, slot, t * P:(t + 1) * P], k_hi[0:QK, slot, t0:t0 + w],
                                     start=True, stop=True)
                last.then_inc(c_mm, 1)

            def turn(h):
                pe.wait_ge(c_max, h * QT + QT)
                for t in range(QT):
                    last = pe.transpose(bank[0:QK + 1, t // 4, t % 4 * P:(t % 4 + 1) * P], row_max[:, t], ident[:, :])
                last.then_inc(x_mm, 1)

            def prepare(h, slot, n):
                if n == 0:
                    keys(h, slot)
                if n == 2:
                    queries(h, slot)
                if n == 4:
                    values(h, slot)
                if n in COARSE:
                    coarse(h, slot, COARSE[n])
                if n == TURN:
                    turn(h)

            def scores(h, slot, n):
                if n == 0:
                    for s in (mk_lo, mq_lo, x_row):
                        pe.wait_ge(s, h + 1)
                half, t = divmod(n, NC)
                x = slice(half * BANK, (half + 1) * BANK)
                t = slice(t * C, (t + 1) * C)
                three(bank[:, 3 + n % 4], k_hi[0:QK + 1, slot, t], k_lo[0:QK + 1, slot, t], q_hi[0:QK + 1, slot, x],
                      q_lo[0:QK + 1, slot, x]).then_inc(s_mm, 1)

            def product(h, slot, n):
                half, t = divmod(n, NC)
                split_done(pe, part_lo, LO_ON, h, n)
                if t == 0:
                    pe.wait_ge(acc_out, h * 2 + half + 1)
                three(bank[:, 7], v_hi[:, slot, t], v_lo[:, slot, t], p_hi[:, n % 4], p_lo[:, n % 4], t == 0,
                      t == NC - 1).then_inc(pv_mm, 1)

            def first():
                pe.wait_ge(pr_lo, 2)
                for n in range(18):
                    prepare(0, 0, n)
                for n in range(AHEAD):
                    scores(0, 0, n)

            def body(h, slot, last):
                for n in range(UNITS):
                    if not (last and n + AHEAD >= UNITS):
                        scores(*after(h, slot, n))
                    product(h, slot, n)
                    if not last:
                        prepare(h + 1, 1 - slot, n)

            over_heads(pe, first, body)

        def mla_scalar(act):
            sq = pr_sq[:, :, :].rearrange("p a b -> p (a b)")
            act.wait_ge(o_lo, 2 * GH)
            act.activation(sq[:, 0:TOK], kv_p, ACT.Square).then_inc(pr_sqd, 1)
            act.wait_ge(pr_mm, 1)
            r = pr_r[:, :]
            link(act, "act", act.activation(r, bank[:, 0:3].rearrange("p a b -> p (a b)")[:, 0:TOK], ACT.Ln,
                                            bias=eps[:, :], scale=1.0 / KVRANK))
            act.activation(r, r, ACT.Exp, scale=-0.5).then_inc(pr_root, 1)
            act.activation(pr_sq[:, :, :], qa_p, ACT.Square).then_inc(pr_sqd, 1)
            act.wait_ge(pr_mul, 1)
            act.activation(kvn_hi[:, :], kv_p, ACT.Copy).then_inc(pr_hi, 1)
            act.wait_ge(pr_mm, 2)
            r = pr_r[:, 0:LAT]
            link(act, "act", act.activation(r, bank[:, 3:5].rearrange("p a b -> p (a b)"), ACT.Ln,
                                            bias=eps[:, :], scale=1.0 / QRANK))
            act.activation(r, r, ACT.Exp, scale=-0.5).then_inc(pr_root, 1)
            act.wait_ge(pr_rot, 4)
            for slot in range(2):
                act.activation(k_hi[NOPE:QK, slot], k_f[NOPE:QK], ACT.Copy).then_inc(pr_khi, 1)
            act.wait_ge(pr_mul, 2)
            act.activation(qn_hi[:, :, :], qa_p, ACT.Copy).then_inc(pr_hi, 1)

            def split(h, slot):
                act.wait_ge(m_w_in[slot], h * 16 + (32 - 16 * slot))
                if not isinstance(h, int):
                    act.wait_ge(mv_mm, h - 1)
                act.activation(wq_hi[:, slot], wq_raw[:, slot], ACT.Copy).then_inc(m_w_hi, 1)
                act.activation(wkv_hi[:, slot], wkv_raw[:, slot], ACT.Copy).then_inc(m_w_hi, 1)

            def prepare(h, slot, n):
                if n == 0:
                    act.wait_ge(mk_mm, h + 1)
                    act.activation(k_hi[0:NOPE, slot], bank[0:NOPE, 0:3].rearrange("p a b -> p (a b)")[:, 0:TOK],
                                   ACT.Copy).then_inc(mk_hi, 1)
                if n == 2:
                    act.wait_ge(mq_mm, h + 1)
                    act.wait_ge(mq_lo, h)
                    act.activation(q_f[0:NOPE], bank[0:NOPE, 0:2].rearrange("p a b -> p (a b)"), ACT.Copy)\
                        .then_inc(mq_raw, 1)
                if n == 3:
                    act.wait_ge(mq_rope, h * 3 + 3)
                    act.wait_ge(mq_raw, h + 1)
                    act.activation(q_hi[0:QK, slot], q_f[0:QK], ACT.Copy).then_inc(mq_hi, 1)
                if n == 4:
                    act.wait_ge(mv_mm, h + 1)
                    src = bank[:, 0:2].rearrange("p a b -> p (a b)")[:, 0:NC * VD].rearrange("p (t v) -> p t v", v=VD)
                    act.activation(v_hi[:, slot, :, VCOL[slot]:VCOL[slot] + VD], src, ACT.Copy).then_inc(mv_hi, 1)
                if n == TURN:
                    act.wait_ge(x_mm, h + 1)
                    act.activation(q_hi[QK:QK + 1, slot], bank[QK:QK + 1, 0:2].rearrange("p a b -> p (a b)"),
                                   ACT.Copy, scale=-1.0).then_inc(x_row, 1)

            def exps(h, n):
                act.wait_ge(s_mm, h * UNITS + (n + 1))
                act.activation(p_f[:, n % 4], bank[:, 3 + n % 4], ACT.Exp, scale=SCALE).then_inc(s_exp, 1)
                if HI_ON[n] == "act":
                    act.wait_ge(s_exp, h * UNITS + (n + 1))
                    act.activation(p_hi[:, n % 4], p_f[:, n % 4], ACT.Copy).then_inc(part_hi["act"], 1)

            def finish(h, slot, half):
                a = h * 2 + half
                act.wait_ge(acc_out, a + 2)
                act.activation(acc_r[NUM[slot]], acc_f[DEN[slot]], ACT.Ln).then_inc(acc_root, 1)
                act.wait_ge(acc_root, a * 2 + 1)
                act.activation(acc_r[NUM[slot]], acc_r[NUM[slot]], ACT.Exp, scale=-1.0).then_inc(acc_root, 1)
                act.wait_ge(acc_div, a + 1)
                act.activation(mixed(mix_hi, h, slot, half), acc_f[NUM[slot]], ACT.Copy).then_inc(acc_hi, 1)

            def first():
                split(0, 0)
                split(1, 1)
                for n in range(18):
                    prepare(0, 0, n)
                for n in range(AHEAD):
                    exps(0, n)

            def body(h, slot, last):
                for n in range(UNITS):
                    g, _, m = after(h, slot, n)
                    if not (last and n + AHEAD >= UNITS):
                        exps(g, m)
                    if n == NC + 1 or n == UNITS - 1:
                        finish(h, slot, 0 if n == NC + 1 else 1)
                    if n == 10 and not isinstance(h, int):
                        split(h + 2, slot)
                    if not last:
                        prepare(h + 1, 1 - slot, n)

            over_heads(act, first, body)

        def mixed(t, h, slot, half):
            x = slice(half * BANK, (half + 1) * BANK)
            if isinstance(h, int):
                return t[NUM[slot], h // 2, x]
            return t[NUM[slot], bass.ds((h - slot) // 2, 1), x].rearrange("p a b -> p (a b)")

        def mla_vector(dve):
            dve.wait_ge(pr_root, 1)
            dve.scalar_tensor_tensor(out=kv_p, in0=kv_p, scalar=qk_norm_sb[:, 2:3], in1=pr_r[:, :], op0=ALU.mult,
                                     op1=ALU.mult).then_inc(pr_mul, 1)
            dve.wait_ge(m_rope, 16)
            rows, sine = slice(NOPE, QK), slice(QK, P)
            dve.tensor_tensor(k_f[rows, 0:LAT], side_p[rows, 0:LAT], rope[rows], ALU.mult).then_inc(pr_rot, 1)
            dve.tensor_tensor(k_rot[rows], side_p[sine, 0:LAT], rope[sine], ALU.mult).then_inc(pr_rot, 1)
            dve.tensor_copy(k_f[rows, LAT:], side_p[rows, LAT:]).then_inc(pr_rot, 1)
            dve.wait_ge(pr_rot, 3)
            dve.tensor_tensor(k_f[rows, 0:LAT], k_f[rows, 0:LAT], k_rot[rows], ALU.add).then_inc(pr_rot, 1)
            dve.wait_ge(pr_hi, 1)
            dve.tensor_tensor(kvn_lo[:, :], kv_p, kvn_hi[:, :].bitcast(F32), ALU.subtract).then_inc(pr_lo, 1)
            dve.wait_ge(pr_root, 2)
            for k in range(2):
                last = dve.scalar_tensor_tensor(out=qa_p[:, k], in0=qa_p[:, k], scalar=qk_norm_sb[:, k:k + 1],
                                                in1=pr_r[:, 0:LAT], op0=ALU.mult, op1=ALU.mult)
            last.then_inc(pr_mul, 1)
            dve.wait_ge(pr_khi, 2)
            for slot in range(2):
                dve.tensor_tensor(k_lo[rows, slot], k_f[rows], k_hi[rows, slot].bitcast(F32), ALU.subtract)\
                    .then_inc(pr_klo, 1)
            dve.wait_ge(pr_hi, 2)
            dve.tensor_tensor(qn_lo[:, :, :], qa_p, qn_hi[:, :, :].bitcast(F32), ALU.subtract).then_inc(pr_lo, 1)
            dve.wait_ge(filled, MLA_FILLS)

            def split(h, slot):
                dve.wait_ge(m_w_hi, h * 2 + 1)
                dve.tensor_tensor(wq_lo[:, slot], wq_raw[:, slot], wq_hi[:, slot].bitcast(F32), ALU.subtract)\
                    .then_inc(m_w_lo, 1)
                dve.wait_ge(m_w_hi, h * 2 + 2)
                dve.tensor_tensor(wkv_lo[:, slot], wkv_raw[:, slot], wkv_hi[:, slot].bitcast(F32), ALU.subtract)\
                    .then_inc(m_w_lo, 1)

            def prepare(h, slot, n):
                two = bank[:, 0:2].rearrange("p a b -> p (a b)")
                if n == 0:
                    dve.wait_ge(mk_hi, h + 1)
                    dve.tensor_tensor(k_lo[0:NOPE, slot], bank[0:NOPE, 0:3].rearrange("p a b -> p (a b)")[:, 0:TOK],
                                      k_hi[0:NOPE, slot].bitcast(F32), ALU.subtract).then_inc(mk_lo, 1)
                if n == 2:
                    dve.wait_ge(mq_mm, h + 1)
                    dve.wait_ge(mq_raw, h + 1)
                    dve.wait_ge(mq_lo, h)
                    dve.tensor_tensor(q_f[rows], two[rows], rope[rows], ALU.mult).then_inc(mq_rope, 1)
                    dve.wait_ge(mq_rope, h * 3 + 1)
                    dve.tensor_tensor(two[rows], two[sine], rope[sine], ALU.mult).then_inc(mq_rope, 1)
                    dve.wait_ge(mq_rope, h * 3 + 2)
                    dve.tensor_tensor(q_f[rows], q_f[rows], two[rows], ALU.add).then_inc(mq_rope, 1)
                if n == 3:
                    dve.wait_ge(mq_hi, h + 1)
                    dve.tensor_tensor(q_lo[0:QK, slot], q_f[0:QK], q_hi[0:QK, slot].bitcast(F32), ALU.subtract)\
                        .then_inc(mq_lo, 1)
                if n == 4:
                    dve.wait_ge(mv_hi, h + 1)
                    cols = slice(VCOL[slot], VCOL[slot] + VD)
                    src = two[:, 0:NC * VD].rearrange("p (t v) -> p t v", v=VD)
                    dve.tensor_tensor(v_lo[:, slot, :, cols], src, v_hi[:, slot, :, cols].bitcast(F32),
                                      ALU.subtract).then_inc(mv_lo, 1)
                if n in COARSE:
                    t = COARSE[n]
                    dve.wait_ge(c_mm, h * QT + (t + 1))
                    dve.tensor_reduce(row_max[:, t, QK:QK + 1], bank[:, 0:3].rearrange("p a b -> p (a b)")[:, 0:TOK],
                                      AX.X, ALU.max).then_inc(c_max, 1)

            def parts(h, n):
                if HI_ON[n] == "dve":
                    dve.wait_ge(s_exp, h * UNITS + (n + 1))
                    dve.tensor_copy(p_hi[:, n % 4], p_f[:, n % 4]).then_inc(part_hi["dve"], 1)
                low(dve, "dve", h, n)

            def gather(h, slot, half):
                a = h * 2 + half
                dve.wait_ge(pv_mm, h * UNITS + (half + 1) * NC)
                dve.wait_ge(acc_lo, a + 1)
                dve.tensor_copy(acc_f[:, :], bank[:, 7]).then_inc(acc_out, 1)

            def finish(h, slot, half):
                a = h * 2 + half
                o = acc_f[NUM[slot]]
                dve.wait_ge(acc_root, a * 2 + 2)
                dve.tensor_tensor(o, o, acc_r[NUM[slot]], ALU.mult).then_inc(acc_div, 1)
                dve.wait_ge(acc_hi, a + 1)
                dve.tensor_tensor(mixed(mix_lo, h, slot, half), o, mixed(mix_hi, h, slot, half).bitcast(F32),
                                  ALU.subtract).then_inc(acc_lo, 1)

            def first():
                split(0, 0)
                split(1, 1)
                for n in range(18):
                    prepare(0, 0, n)
                for n in range(AHEAD):
                    parts(0, n)

            def body(h, slot, last):
                for n in range(UNITS):
                    g, _, m = after(h, slot, n)
                    if not (last and n + AHEAD >= UNITS):
                        parts(g, m)
                    if n == NC - 1 or n == UNITS - 1:
                        gather(h, slot, n // NC)
                    if n == NC + 1 or n == UNITS - 1:
                        finish(h, slot, 0 if n == NC + 1 else 1)
                    if n == 10 and not isinstance(h, int):
                        split(h + 2, slot)
                    if not last:
                        prepare(h + 1, 1 - slot, n)

            over_heads(dve, first, body)

        def wo_tiles(eng, tile):
            tile(0, 0)
            tile(1, 1)
            with eng.Fori(0, 3) as i:
                for slot in range(2):
                    tile(i * 2 + (2 + slot), slot)

        def wo_sync(sp):
            sp.wait_ge(pv_mm, HEADS * UNITS)
            def load(t, slot):
                if not isinstance(t, int):
                    sp.wait_ge(wo_split_lo, t - 1)
                sp.dma_start(wo_raw[:, slot], w_out[bass.ds(t, 1)].rearrange("a p k m -> p (a k) m"))\
                    .then_inc(w_in_sem[slot], 16)

            def loads(t, slot):
                load(t, slot)
                for k in range(4):
                    ada_load(sp, ada_c, t * 4 + k, k)
            ada_cond(sp, ada_c)
            wo_tiles(sp, loads)

        def wo_scalar(act):
            def split(t, slot):
                act.wait_ge(w_in_sem[slot], t * 8 + (16 * 8 + 16 - 8 * slot))
                if not isinstance(t, int) or t >= 2:
                    act.wait_ge(wo_mm, t - 1)
                act.activation(wo_hi[:, slot], wo_raw[:, slot], ACT.Copy).then_inc(wo_split_hi, 1)

            def leave(t, slot):
                act.wait_ge(wo_mm, t + 1)
                act.activation(room2.res[:, bass.ds(t, 1)].rearrange("p a b -> p (a b)"),
                               bank[:, 2 * slot:2 * slot + 2].rearrange("p a b -> p (a b)"), ACT.Copy)\
                    .then_inc(wo_out, 1)

            split(0, 0)
            split(1, 1)
            ada_silu(act, ada_c)
            with act.Fori(0, 3) as i:
                for slot in range(2):
                    leave(i * 2 + slot, slot)
                    split(i * 2 + (2 + slot), slot)
            leave(6, 0)
            leave(7, 1)

        def wo_vector(dve):
            def split(t, slot):
                dve.wait_ge(wo_split_hi, t + 1)
                dve.tensor_tensor(wo_lo[:, slot], wo_raw[:, slot], wo_hi[:, slot].bitcast(F32),
                                  ALU.subtract).then_inc(wo_split_lo, 1)

            split(0, 0)
            for n in range(ada_c.tiles):
                if n % 4 == 0 and n // 4 + 1 < DK:
                    split(n // 4 + 1, (n // 4 + 1) % 2)
                ada_tile(dve, ada_c, n)
            ada_finish(dve, ada_c, (2,), (1, 2))

        def wo_tensor(pe):
            pe.wait_ge(acc_lo, 2 * HEADS + 1)
            pe.wait_ge(o_lo, 2 * GH)
            def tile(t, slot):
                pe.wait_ge(wo_split_lo, t + 1)
                if not isinstance(t, int):
                    pe.wait_ge(wo_out, t - 1)
                for c in range(2):
                    x = slice(c * BANK, (c + 1) * BANK)
                    for k in range(DK):
                        acc = bank[:, 2 * slot + c]
                        pe.matmul(acc, wo_hi[:, slot, k], mix_hi[:, k, x], start=(k == 0), stop=False)
                        pe.matmul(acc, wo_hi[:, slot, k], mix_lo[:, k, x], start=False, stop=False)
                        last = pe.matmul(acc, wo_lo[:, slot, k], mix_hi[:, k, x], start=False, stop=(k == DK - 1))
                last.then_inc(wo_mm, 1)
            wo_tiles(pe, tile)

        def y_added(eng, f):
            def wait(c, k):
                eng.wait_ge(f.y_add, 2 + (PAIRS - 1) * DK * len(f.chunks) + c * DK + k + 1)
            return wait

        @block.sync
        def _(sp):
            ada_cond(sp, ada_a)
            for t in range(4):
                ada_load(sp, ada_a, t, t)
            for t, s in ((bada_sb, b_ada), (pre_sb, pre), (post_sb, post), (ident, ident_d),
                         (mask_raw, mask_d), (wa_sb, w_a), (ba_sb, b_a), (gnorm_sb, g_norm),
                         (qk_norm_sb, qk_norm)):
                sp.dma_start(t[:], s).then_inc(consts_in, 16)
            norm_sync(sp, n1)
            with sp.Fori(0, ada_a.tiles // 4 - 1) as i:
                for k in range(4):
                    ada_load(sp, ada_a, i * 4 + (4 + k), k)

            def loads_b():
                sp.wait_ge(n1.lo, DK * 3)
                ada_cond(sp, ada_b)
                for t in range(4):
                    ada_load(sp, ada_b, t, t)
                with sp.Fori(0, ada_b.tiles // 4 - 1) as i:
                    for k in range(4):
                        ada_load(sp, ada_b, i * 4 + (4 + k), k)
            ffn_sync(sp, f1, loads_b)
            norm_sync(sp, n2, lambda: sp.wait_ge(f1.half, 2 * FJ))
            sp.wait_ge(n2.stored, 16 * 3)
            proj_sync(sp)
            mla_sync(sp)
            wo_sync(sp)
            sp.wait_ge(acc_lo, 2 * HEADS + 1)
            norm_sync(sp, n3, lambda: sp.wait_ge(wo_mm, 1))
            sp.wait_ge(n3.stored, 16 * 2)
            ffn_sync(sp, f2)
            norm_sync(sp, n4, lambda: sp.wait_ge(f2.half, 2 * FJ))
            sp.wait_ge(n4.stored, 16 * 2)

        @block.gpsimd
        def _(pool):
            pool.memset(ones[:, :], 1.0).then_inc(filled, 1)
            pool.memset(eps[:, :], EPS).then_inc(filled, 1)
            pool.wait_ge(consts_in, CONSTS)
            pool.tensor_copy(mask[:, :, :].rearrange("p l (r c) -> p l r c", c=C),
                             mask_raw[:, :, :].rearrange("p l (r c) -> p l r c", r=1)
                             .to_broadcast([P, LEVELS, BANK // C, C])).then_inc(filled, 1)
            pool.wait_ge(gains_done, 2)
            pool.memset(room1.res[:, :, :], 0.0).then_inc(f1.y_add, 2)
            norm_pool(pool, n2)
            gla_pool(pool)
            mla_pool(pool)
            norm_pool(pool, n3)
            pool.wait_ge(n3.lo, DK * 2)
            pool.wait_ge(n3.stored, 16 * 2)
            pool.memset(room2.res[:, :, :], 0.0).then_inc(f2.y_add, 2)
            norm_pool(pool, n4)

        @block.scalar
        def _(act):
            ada_silu(act, ada_a)
            act.wait_ge(filled, CONST_FILLS)
            norm_scalar(act, n1)
            ffn_scalar(act, f1, lambda: ada_silu(act, ada_b))
            norm_scalar(act, n2, y_added(act, f1))
            proj_scalar(act)
            gla_scalar(act)
            mla_scalar(act)
            wo_scalar(act)
            norm_scalar(act, n3, lambda c, k: act.wait_ge(wo_out, k + 1))
            ffn_scalar(act, f2)
            norm_scalar(act, n4, y_added(act, f2))

        @block.tensor
        def _(pe):
            pe.wait_ge(filled, CONST_FILLS)
            norm_tensor(pe, n1)
            ffn_tensor(pe, f1)
            norm_tensor(pe, n2, lambda: pe.wait_ge(f1.y_add, 2 + PAIRS * DK * len(CHUNKS)))
            proj_tensor(pe)
            gla_tensor(pe)
            mla_tensor(pe)
            wo_tensor(pe)
            norm_tensor(pe, n3)
            ffn_tensor(pe, f2)
            norm_tensor(pe, n4, lambda: pe.wait_ge(f2.y_add, 2 + PAIRS * DK * 2))

        @block.vector
        def _(dve):
            dve.wait_ge(consts_in, CONSTS)
            for t in range(ada_a.tiles):
                ada_tile(dve, ada_a, t)
            ada_finish(dve, ada_a, (0,), ())
            norm_vector(dve, n1)
            tiles = iter(range(ada_b.tiles))

            def more():
                for _, t in zip(range(ada_b.tiles // 3), tiles):
                    ada_tile(dve, ada_b, t)
                    if t == ada_b.tiles - 1:
                        ada_finish(dve, ada_b, (1,), (0,))
            ffn_vector(dve, f1, more)
            norm_vector(dve, n2)
            proj_vector(dve)
            gla_vector(dve)
            mla_vector(dve)
            wo_vector(dve)
            norm_vector(dve, n3)
            ffn_vector(dve, f2)
            norm_vector(dve, n4)


ORDER_IN = ["x_t", "cond", "w_ada", "b_ada", "pre", "post", "f1_in", "f1_out", "f2_in", "f2_out", "w_in", "w_a", "b_a",
            "g_norm", "ident", "mask", "w_qb", "w_kvb", "qk_norm", "rope", "w_out"]


def rotated(first):
    c = np.arange(first, first + ROPE)
    return np.concatenate([c[8:16], c[0:8], c[24:32], c[16:24]])


def lay_out(x, c, ctx, c_ctx, w_ada, b_ada, norm_pre, norm_post, ffn1_w_in, ffn1_w_out, ffn2_w_in, ffn2_w_out, w_in,
            mla_q_norm, mla_w_qb, mla_kv_norm, mla_w_kvb, gla_w_a_fwd, gla_b_a_fwd, gla_w_a_bwd, gla_b_a_bwd,
            gla_norm, w_out):
    a = {"x_t": np.concatenate([x[0], ctx[0]]).T.reshape(DK, P, TOK).transpose(1, 0, 2)}
    a["cond"] = np.stack([c[0], c_ctx])
    a["w_ada"] = w_ada[0].T.reshape(9 * DK, P, D)
    a["b_ada"] = np.repeat(b_ada[0].reshape(9, DK, P, 1).transpose(2, 0, 1, 3), 2, -1)
    a["pre"] = np.repeat(norm_pre[0].reshape(3, DK, P, 1).transpose(2, 0, 1, 3), 2, -1)
    a["post"] = np.repeat(norm_post[0].reshape(3, DK, P, 1).transpose(2, 0, 1, 3), 2, -1)
    for f, w1, w2 in (("f1", ffn1_w_in, ffn1_w_out), ("f2", ffn2_w_in, ffn2_w_out)):
        a[f + "_in"] = w1[0].reshape(DK, P, 2, FJ, P).transpose(3, 2, 1, 0, 4).reshape(2 * FJ, P, DK, P)
        a[f + "_out"] = w2[0].reshape(FJ, P, D)
    at = np.cumsum([0, QRANK, KVRANK, ROPE, GH * GDK, GH * GDK, GH * GDV, GH * GDV, 2 * GRANK])
    part = [np.arange(at[i], at[i + 1]) for i in range(8)]
    cols = np.concatenate([part[1], part[7], part[2], part[2], rotated(at[2]), part[4], part[5], part[0], part[3],
                           part[6]])
    a["w_in"] = w_in[0][:, cols].reshape(DK, P, 16, P).transpose(2, 1, 0, 3)
    w_a = np.zeros((2 * GRANK, 4, P), w_in.dtype)
    w_a[:GRANK, 0:2] = gla_w_a_fwd[0].reshape(GRANK, 2, P)
    w_a[GRANK:, 2:4] = gla_w_a_bwd[0].reshape(GRANK, 2, P)
    a["w_a"] = w_a
    a["b_a"] = np.concatenate([gla_b_a_fwd[0], gla_b_a_bwd[0]]).reshape(4, P).T
    a["g_norm"] = gla_norm[0].reshape(P, 1)
    a["ident"] = np.eye(P, dtype=np.float32)
    i = np.arange(C)
    same = np.stack([i[:, None] // b == i[None] // b for b in [C >> k for k in range(1, LEVELS + 1)]], 1)
    a["mask"] = same.astype(np.float32)
    heads = np.concatenate([np.concatenate([np.arange(h * QK, (h + 1) * QK), rotated(h * QK + NOPE)])
                            for h in range(HEADS)])
    a["w_qb"] = mla_w_qb[0][:, heads].reshape(2, P, HEADS, P).transpose(2, 1, 0, 3)
    a["w_kvb"] = mla_w_kvb[0].reshape(P, HEADS, P).transpose(1, 0, 2)
    a["qk_norm"] = np.stack([mla_q_norm[0][:P], mla_q_norm[0][P:], mla_kv_norm[0]], 1)
    a["rope"] = rope_table()
    a["w_out"] = w_out[0].reshape(DK, P, DK, P).transpose(2, 1, 0, 3)
    return {n: np.ascontiguousarray(v) for n, v in a.items()}


def rope_table():
    t = np.arange(LAT, dtype=np.float32)
    freq = (np.float32(10000.0) ** (-np.arange(0, ROPE // 2, 2, dtype=np.float32) / np.float32(ROPE // 2)))
    row, col = np.floor(t / GRID_W).astype(np.float32), (t % GRID_W).astype(np.float32)
    ang = np.concatenate([row * freq[:, None]] * 2 + [col * freq[:, None]] * 2)
    sign = np.where(np.arange(ROPE) % 16 < 8, -1, 1).astype(np.float32)[:, None]
    table = np.zeros((P, LAT), np.float32)
    table[NOPE:QK] = np.cos(ang)
    table[QK:] = np.sin(ang) * sign
    return table


def kernel(**inputs):
    import concourse.bacc as bacc
    from concourse.bass_utils import run_bass_kernel_spmd

    nc = bacc.Bacc("TRN2", target_bir_lowering=False, num_devices=1)
    a = lay_out(**{n: np.asarray(v) for n, v in inputs.items()})
    arrays = {f"in_{n}": a[n] for n in ORDER_IN}
    args = [nc.dram_tensor(n, v.shape, mybir.dt.from_np(v.dtype), kind="ExternalInput").ap()
            for n, v in arrays.items()]
    x1 = nc.dram_tensor("x1", (P, DK, TOK), F32, kind="Internal").ap()
    x2 = nc.dram_tensor("x2", (P, DK, LAT), F32, kind="Internal").ap()
    out = nc.dram_tensor("out", (P, DK, LAT), F32, kind="ExternalOutput").ap()
    build(nc, *args, x1, x2, out)
    r = run_bass_kernel_spmd(nc, [arrays], core_ids=[0])
    y = r.results[0]["out"]
    return y.transpose(1, 0, 2).reshape(D, LAT).T.reshape(1, LAT, D)
```

```python
from contextlib import ExitStack

import numpy as np

import concourse.bass as bass
from concourse import mybir

P = 128
D = 1024
DK = D // P
LAT = 1024
CTX = 256
TOK = LAT + CTX
FF = 2816
FJ = FF // P
HEADS, NOPE, ROPE, VD = 8, 64, 32, 64
QK = NOPE + ROPE
QRANK, KVRANK = 256, 128
GH, GDK, GDV, GRANK = 4, 64, 128, 16
GRID_W = 64
EPS = 1e-6
GATE_NORM = 16.0
C = 128
NC_LAT, NC_CTX = LAT // C, CTX // C
NC = NC_LAT + NC_CTX
BANK = 512
LEVELS = 7

F32 = mybir.dt.float32
F32R = mybir.dt.float32r
U8 = mybir.dt.uint8
ACT = mybir.ActivationFunctionType
ALU = mybir.AluOpType
AX = mybir.AxisListType

CHUNKS = [(0, 512, 0), (512, 512, 0), (1024, 256, 1)]


def build(nc, x_t, cond, w_ada, b_ada, pre, post, f1_in, f1_out, f2_in, f2_out, w_in, w_a, b_a, g_norm, ident_d, mask_d, w_qb, w_kvb, qk_norm,
          rope_d, w_out, x1_d, x2_d, out):
    with ExitStack() as ctx:
        def sem(name):
            return ctx.enter_context(nc.semaphore(name))

        base = -(-nc.sbuf_base // 32) * 32
        end = nc.sbuf_base + nc.sbuf_bytes_remaining
        plan = {"at": base}

        def put(name, shape, dt, at=None):
            size = int(np.prod(shape[1:])) * (1 if dt == U8 else 4)
            at = plan["at"] if at is None else at
            t = nc.alloc_sbuf_tensor_at(name, list(shape), dt, offset=at)
            plan["at"] = at + -(-size // 32) * 32
            assert plan["at"] <= end, (name, plan["at"] - end)
            return t

        bank = ctx.enter_context(nc.psum_tensor("bank", [P, 8, BANK], F32))

        ones = put("ones", [P, P], F32)
        eps = put("eps", [P, 1], F32)
        mods = put("mods", [P, 9, DK, 2], F32)
        bada_sb = put("bada_sb", [P, 9, DK, 2], F32)
        pre_sb = put("pre_sb", [P, 3, DK, 2], F32)
        post_sb = put("post_sb", [P, 3, DK, 2], F32)
        gain_pre = put("gain_pre", [P, 3, DK, 2], F32)
        gain_post = put("gain_post", [P, 3, DK, 2], F32)
        ident = put("ident", [P, P], F32)
        wa_sb = put("wa_sb", [2 * GRANK, 4, P], F32)
        ba_sb = put("ba_sb", [P, 4], F32)
        gnorm_sb = put("gnorm_sb", [P, 1], F32)
        qk_norm_sb = put("qk_norm_sb", [P, 3], F32)
        mask = put("mask", [P, LEVELS, BANK], U8)
        arena = plan["at"]

        class Ada:
            def __init__(self, n, first, tiles, conds, before, at):
                self.first, self.tiles, self.conds = first, tiles, conds
                self.before, self.after = before, before + tiles * conds
                self.cond = put(f"{n}_cond", [P, 2, D], F32, at=at)
                self.w = put(f"{n}_w", [P, 4, D], F32)
                self.junk = put(f"{n}_junk", [P, 2, D], F32)

        ada_a = Ada("ada_a", 0, 2 * DK, 2, 0, arena + DK * TOK * 4)
        mask_raw = put("mask_raw", [P, LEVELS, C], F32)
        ada_b = Ada("ada_b", 2 * DK, 3 * DK, 2, ada_a.after, arena)
        assert plan["at"] <= arena + DK * TOK * 4

        class Room:
            def stream(self, n, at):
                self.a_hi = put(f"{n}_a_hi", [P, DK, self.tok], F32R, at=at)
                self.a_lo = put(f"{n}_a_lo", [P, DK, self.tok], F32R)

            def norm(self, n, at, rstd=None, xin=True):
                plan["at"] = at
                if xin:
                    self.xin = put(f"{n}_xin", [P, DK, BANK], F32)
                self.sq = put(f"{n}_sq", [P, 4, BANK], F32)
                self.tmp = put(f"{n}_tmp", [P, 2, BANK], F32)
                self.rstd = rstd or put(f"{n}_rstd", [P, 2, BANK], F32)

            def hidden(self, n, at):
                self.w1_raw = put(f"{n}_w1_raw", [P, 2, DK, P], F32, at=at)
                self.w1_hi = put(f"{n}_w1_hi", [P, 2, DK, P], F32R)
                self.w1_lo = put(f"{n}_w1_lo", [P, 2, DK, P], F32R)
                self.w2_raw = put(f"{n}_w2_raw", [P, D], F32)
                self.u_f = put(f"{n}_u_f", [P, self.tok], F32)
                self.kept = plan["at"]
                self.w2_hi = put(f"{n}_w2_hi", [P, 2, D], F32R)
                self.w2_lo = put(f"{n}_w2_lo", [P, 2, D], F32R)
                self.hidden_at = plan["at"]
                self.u_hi = put(f"{n}_u_hi", [P, 3, self.tok], F32R)
                self.u_lo = put(f"{n}_u_lo", [P, 3, self.tok], F32R)

        room1 = Room()
        room1.tok = TOK
        room1.res = put("r1_res", [P, DK, TOK], F32, at=arena)
        room1.stream("r1", plan["at"])
        scratch = plan["at"]
        room1.hidden("r1", scratch)
        room1.norm("r1", scratch)
        assert plan["at"] <= room1.kept
        room0 = Room()
        room0.tok, room0.res, room0.a_hi, room0.a_lo = TOK, room1.res, room1.a_hi, room1.a_lo
        room0.norm("r0", room1.hidden_at, xin=False)

        wp_raw = put("wp_raw", [P, 2, DK, P], F32, at=room1.kept)
        wp_hi = put("wp_hi", [P, 2, DK, P], F32R)
        wp_lo = put("wp_lo", [P, 2, DK, P], F32R)
        pr_sq = put("pr_sq", [P, 2, LAT], F32)
        pr_r = put("pr_r", [P, TOK], F32)
        proj_c = put("proj_c", [P, 8, TOK], F32, at=arena)
        free1 = plan["at"]
        proj_l = put("proj_l", [P, 8, LAT], F32, at=free1 + 2 * DK * TOK * 4)
        free2 = plan["at"]
        kv_p, side_p, gk_p, gv_p = proj_c[:, 0], proj_c[:, 1], proj_c[:, 2:4], proj_c[:, 4:8]
        qa_p, gq_p, gg_p = proj_l[:, 0:2], proj_l[:, 2:4], proj_l[:, 4:8]

        cum = put("cum", [P, 4, TOK], F32, at=free1)
        v_tok = put("v_tok", [P, NC, GH, GDV], F32)
        state = put("state", [P, 4, NC, GDV], F32)
        attn = put("attn", [P, GH, NC_LAT, C], F32)
        decay = put("decay", [P, 4, NC], F32)
        assert plan["at"] <= free1 + 2 * DK * TOK * 4
        keep = put("keep", [P, TOK + 1], F32, at=free2)
        share = plan["at"]
        z = put("z", [P, 2, TOK], F32)
        zl = put("zl", [P, 2, TOK], F32)
        kd = put("kd", [P, 2, TOK], F32, at=share)
        kd_tok = put("kd_tok", [P, 2, NC, C], F32)
        diff = put("diff", [P, 2, 2, LAT], F32, at=share)
        q_lev = put("q_lev", [P, 2, LAT], F32)
        k_lev = put("k_lev", [P, 2, LAT], F32)
        q_dec = put("q_dec", [P, 4, LAT], F32, at=share)
        o_gla_at = plan["at"]
        o_gla = put("o_gla", [P, GH, LAT], F32)
        g_sq = put("g_sq", [P, 2, BANK], F32)
        g_rstd = put("g_rstd", [P, 2, BANK], F32)
        mix_hi = put("mix_hi", [P, DK, LAT], F32R, at=arena + 2 * TOK * 4)
        mix_lo = put("mix_lo", [P, DK, LAT], F32R)
        after_mix = plan["at"]

        kvn_hi = put("kvn_hi", [P, TOK], F32R)
        kvn_lo = put("kvn_lo", [P, TOK], F32R)
        qn_hi = put("qn_hi", [P, 2, LAT], F32R)
        qn_lo = put("qn_lo", [P, 2, LAT], F32R)
        k_hi = put("k_hi", [P, 2, TOK], F32R)
        k_lo = put("k_lo", [P, 2, TOK], F32R)
        assert plan["at"] <= free1 + 2 * DK * TOK * 4
        q_f = put("q_f", [P, LAT], F32)
        q_hi = put("q_hi", [P, 2, LAT], F32R)
        q_lo = put("q_lo", [P, 2, LAT], F32R)
        v_at = plan["at"]
        v_hi = put("v_hi", [P, 2, NC, P], F32R)
        v_lo = put("v_lo", [P, 2, NC, P], F32R)
        p_at = plan["at"]
        rope = put("rope", [P, LAT], F32)
        vt_lat = rope[0:VD]
        wq_raw = put("wq_raw", [P, 2, 2, P], F32)
        wq_hi = put("wq_hi", [P, 2, 2, P], F32R)
        wq_lo = put("wq_lo", [P, 2, 2, P], F32R)
        wkv_raw = put("wkv_raw", [P, 2, P], F32)
        wkv_hi = put("wkv_hi", [P, 2, P], F32R)
        wkv_lo = put("wkv_lo", [P, 2, P], F32R)
        assert plan["at"] <= o_gla_at
        p_f = put("p_f", [P, 4, BANK], F32, at=o_gla_at)
        p_hi = put("p_hi", [P, 4, BANK], F32R)
        p_lo = put("p_lo", [P, 4, BANK], F32R)
        k_f = put("k_f", [P, TOK], F32, at=v_at)
        k_rot = put("k_rot", [P, LAT], F32)
        assert plan["at"] <= p_at
        acc_f = put("acc_f", [P, BANK], F32, at=arena)
        acc_r = put("acc_r", [P, BANK], F32)
        row_max = put("row_max", [P, LAT // P, QK + 1], F32)
        vt_ctx = put("vt_ctx", [P, CTX], F32)
        assert plan["at"] <= arena + 2 * TOK * 4

        room2 = Room()
        room2.tok = LAT
        room2.hidden("r2", arena)
        assert plan["at"] <= after_mix
        room2.stream("r2", plan["at"])
        assert plan["at"] >= after_mix
        room2_res = plan["at"]
        room2.res = put("r2_res", [P, DK, LAT], F32)
        room2.norm("r2", plan["at"], rstd=room2.u_f[:, :].rearrange("p (a b) -> p a b", b=BANK))
        wo_raw = put("wo_raw", [P, 2, DK, P], F32, at=after_mix)
        wo_hi = put("wo_hi", [P, 2, DK, P], F32R)
        wo_lo = put("wo_lo", [P, 2, DK, P], F32R)
        ada_c = Ada("ada_c", 5 * DK, 4 * DK, 1, ada_b.after, plan["at"])
        assert plan["at"] <= room2_res

        link_sem = {n: sem(f"{n}_link") for n in ("dve", "act", "pool")}
        count = {n: 0 for n in link_sem}

        def link(eng, name, ins):
            count[name] += 1
            ins.then_inc(link_sem[name], 1)
            eng.wait_ge(link_sem[name], count[name])

        consts_in = sem("consts_in")
        CONSTS = 16 * 9
        filled = sem("filled")
        CONST_FILLS, SCAN_FILLS, MLA_FILLS = 3, 5, 13
        ada_in = [sem(f"ada_in{i}") for i in range(4)]
        cond_in = sem("cond_in")
        cond_silu = sem("cond_silu")
        ada_mul = sem("ada_mul")
        gains_done = sem("gains_done")

        EXP_LN = "natural_log_exp_and_others"

        class Norms:
            def __init__(self, n, room, chunks, steps, post_s, pre_s, source, target, overlapped=False):
                self.overlapped = overlapped
                self.room, self.chunks, self.steps = room, chunks, steps
                self.post_s, self.pre_s, self.source, self.target = post_s, pre_s, source, target
                if self.posts():
                    self.x_in = sem(f"{n}_x_in")
                    self.added = (sem(f"{n}_added_even"), sem(f"{n}_added_odd"))
                    self.stored = sem(f"{n}_stored")
                else:
                    self.x_in = [sem(f"{n}_x_in{c}") for c in range(len(chunks))]
                if len(steps) > len(self.posts()):
                    self.hi = sem(f"{n}_hi")
                    self.lo = sem(f"{n}_lo")
                self.squared = sem(f"{n}_squared")
                self.stat = sem(f"{n}_stat")
                self.rooted = sem(f"{n}_rooted")
                self.scaled = sem(f"{n}_scaled")

            def posts(self):
                return [c for kind, c in self.steps if kind == "post"]

        PARTS = (ada_a, ada_b, ada_c)

        def ada_cond(sp, a):
            sp.dma_start(a.cond[:, 0:a.conds], cond[0:a.conds].partition_broadcast(P)).then_inc(cond_in, 16)

        def ada_load(sp, a, t, slot):
            if not isinstance(t, int) or t >= 4:
                sp.wait_ge(ada_mul, t * a.conds + (a.before - 3 * a.conds))
            sp.dma_start(a.w[:, slot], w_ada[bass.ds(t + a.first, 1)].rearrange("a p k -> p (a k)"))\
                .then_inc(ada_in[slot], 16)

        def ada_silu(act, a):
            m = PARTS.index(a)
            act.wait_ge(cond_in, 16 * (m + 1))
            act.activation(a.cond[:, 0:a.conds], a.cond[:, 0:a.conds], ACT.Silu).then_inc(cond_silu, 1)

        def ada_tile(dve, a, t):
            if t == 0:
                dve.wait_ge(cond_silu, PARTS.index(a) + 1)
            dve.wait_ge(ada_in[t % 4], 16 * ((a.first + t) // 4 + 1))
            m, k = divmod(a.first + t, DK)
            for c in range(a.conds):
                n = a.before + t * a.conds + c
                if n >= 2:
                    dve.wait_ge(ada_mul, n - 1)
                dve.tensor_tensor_reduce(out=a.junk[:, n % 2], in0=a.w[:, t % 4], in1=a.cond[:, c], scale=1.0,
                                         scalar=0.0, op0=ALU.mult, op1=ALU.add,
                                         accum_out=mods[:, m, k, c:c + 1]).then_inc(ada_mul, 1)

        def ada_finish(dve, a, pre, post):
            m0, m1, w = a.first // DK, (a.first + a.tiles) // DK, slice(0, a.conds)
            dve.wait_ge(ada_mul, a.after)
            link(dve, "dve", dve.tensor_tensor(mods[:, m0:m1, :, w], mods[:, m0:m1, :, w], bada_sb[:, m0:m1, :, w],
                                               ALU.add))
            for s in pre:
                last = dve.scalar_tensor_tensor(out=gain_pre[:, s, :, w], in0=mods[:, 3 * s + 1, :, w], scalar=1.0,
                                                in1=pre_sb[:, s, :, w], op0=ALU.add, op1=ALU.mult)
            for s in post:
                last = dve.scalar_tensor_tensor(out=gain_post[:, s, :, w], in0=mods[:, 3 * s + 2, :, w],
                                                scalar=1.0 if s == 1 else 0.5, in1=post_sb[:, s, :, w],
                                                op0=ALU.mult, op1=ALU.mult)
            last.then_inc(gains_done, 1)
            dve.wait_ge(gains_done, PARTS.index(a) + 1)

        def chunks_added(eng, q, m):
            eng.wait_ge(q.added[0], m * (DK // 2))
            eng.wait_ge(q.added[1], m * (DK // 2))

        def norm_sync(sp, q, ready=None, early=lambda: None):
            posts = q.posts()
            if not posts:
                for c, (t0, w, _) in enumerate(q.chunks):
                    sp.dma_start(q.room.res[:, :, t0:t0 + w], q.source[:, :, t0:t0 + w]).then_inc(q.x_in[c], 16)
                return
            ready()

            def store(m):
                t0, w, _ = q.chunks[posts[m]]
                chunks_added(sp, q, m + 1)
                sp.dma_start(q.target[:, :, t0:t0 + w], q.room.res[:, :, t0:t0 + w]).then_inc(q.stored, 16)

            for m, c in enumerate(posts):
                t0, w, _ = q.chunks[c]
                if m:
                    chunks_added(sp, q, m)
                sp.dma_start(q.room.xin[:, :, 0:w], q.source[:, :, t0:t0 + w]).then_inc(q.x_in, 16)
                if m:
                    store(m - 1)
                else:
                    early()
            store(len(posts) - 1)

        def norm_bank(q, n):
            return 0 if q.overlapped and n == 0 else 6 + n % 2

        def norm_step(pe, q, n):
            w = q.chunks[q.steps[n][1]][1]
            for k in range(DK):
                pe.wait_ge(q.squared, n * DK + k + 1)
                if n >= 2 and k == 0:
                    pe.wait_ge(q.rooted, n - 1)
                pe.matmul(bank[:, norm_bank(q, n), 0:w], ones[:, :], q.room.sq[:, k % 4, 0:w], start=(k == 0),
                          stop=(k == DK - 1)).then_inc(q.stat, 1)

        def norm_tensor(pe, q, bank_free=None):
            if bank_free:
                bank_free()
            for n in range(1 if q.overlapped else 0, len(q.steps)):
                norm_step(pe, q, n)

        def norm_scalar(act, q, y_ready=None, early=lambda: None, late_highs=False):
            act.preload_act_table_set(EXP_LN)
            room, waiting = q.room, []

            def highs(c):
                act.wait_ge(gains_done, q.pre_s + 1)
                t0, w, which = q.chunks[c]
                for k in range(DK):
                    act.wait_ge(q.scaled, q.steps.index(("pre", c)) * DK + k + 1)
                    act.activation(room.a_hi[:, k, t0:t0 + w], room.tmp[:, k % 2, 0:w], ACT.Identity,
                                   bias=mods[:, 3 * q.pre_s, k, which:which + 1]).then_inc(q.hi, 1)

            for n, (kind, c) in enumerate(q.steps):
                t0, w, which = q.chunks[c]
                for k in range(DK):
                    if kind == "post":
                        y_ready(c, k)
                    elif q.posts():
                        act.wait_ge(q.added[k % 2], q.posts().index(c) * (DK // 2) + k // 2 + 1)
                    else:
                        act.wait_ge(q.x_in[c], 16)
                    if n * DK + k >= 4:
                        act.wait_ge(q.stat, n * DK + k - 3)
                    act.activation(room.sq[:, k % 4, 0:w], room.res[:, k, t0:t0 + w], ACT.Square)\
                        .then_inc(q.squared, 1)
                act.wait_ge(q.stat, (n + 1) * DK)
                if n >= 2:
                    act.wait_ge(q.scaled, (n - 1) * DK)
                r = room.rstd[:, n % 2, 0:w]
                link(act, "act", act.activation(r, bank[:, norm_bank(q, n), 0:w], ACT.Ln, bias=eps[:, :], scale=1.0 / D))
                act.activation(r, r, ACT.Exp, scale=-0.5).then_inc(q.rooted, 1)
                if n == 1:
                    early()
                if kind == "pre":
                    waiting.append(c)
                if waiting and not (late_highs and kind == "pre" and len(waiting) == 1):
                    highs(waiting.pop(0))
            for c in waiting:
                highs(c)

        def norm_vector(dve, q, early=lambda: None):
            room, pres = q.room, 0
            for n, (kind, c) in enumerate(q.steps):
                t0, w, which = q.chunks[c]
                dve.wait_ge(q.rooted, n + 1)
                gain = gain_post[:, q.post_s] if kind == "post" else gain_pre[:, q.pre_s]

                def low(k):
                    dve.wait_ge(q.hi, pres * DK + k + 1)
                    dve.scalar_tensor_tensor(out=room.a_lo[:, k, t0:t0 + w], in0=room.tmp[:, k % 2, 0:w],
                                             scalar=mods[:, 3 * q.pre_s, k, which:which + 1],
                                             in1=room.a_hi[:, k, t0:t0 + w].bitcast(F32), op0=ALU.add,
                                             op1=ALU.subtract).then_inc(q.lo, 1)

                def add(k):
                    dve.wait_ge(q.x_in, 16 * (q.posts().index(c) + 1))
                    dve.wait_ge(q.scaled, n * DK + k + 1)
                    y = room.res[:, k, t0:t0 + w]
                    dve.tensor_tensor(y, y, room.xin[:, k, 0:w], ALU.add).then_inc(q.added[1], 1)

                for k in range(DK):
                    y = room.res[:, k, t0:t0 + w]
                    if kind == "pre" and k >= 2:
                        low(k - 2)
                        dve.wait_ge(q.lo, pres * DK + k - 1)
                    elif kind == "pre" and pres:
                        dve.wait_ge(q.lo, pres * DK)
                    dve.scalar_tensor_tensor(out=y if kind == "post" else room.tmp[:, k % 2, 0:w], in0=y,
                                             scalar=gain[:, k, which:which + 1], in1=room.rstd[:, n % 2, 0:w],
                                             op0=ALU.mult, op1=ALU.mult).then_inc(q.scaled, 1)
                    if kind == "post" and k % 2 == 0 and k:
                        add(k - 1)
                if kind == "post":
                    add(DK - 1)
                if kind == "pre":
                    low(DK - 2)
                    low(DK - 1)
                    pres += 1
                if n == 1:
                    early()

        def norm_pool(pool, q):
            for m, c in enumerate(q.posts()):
                t0, w, _ = q.chunks[c]
                n = q.steps.index(("post", c))
                pool.wait_ge(q.x_in, 16 * (m + 1))
                for k in range(0, DK, 2):
                    pool.wait_ge(q.scaled, n * DK + k + 1)
                    y = q.room.res[:, k, t0:t0 + w]
                    pool.tensor_tensor(y, y, q.room.xin[:, k, 0:w], ALU.add).then_inc(q.added[0], 1)

        class Ffn:
            def __init__(self, n, s, room, chunks, norms):
                self.s, self.room, self.chunks, self.norms = s, room, chunks, norms
                self.tok = sum(w for _, w, _ in chunks)
                self.w_in, self.w_out = (f1_in, f1_out) if s == 0 else (f2_in, f2_out)
                self.w1_in = [sem(f"{n}_w1_in{i}") for i in range(2)]
                self.w2_in = sem(f"{n}_w2_in")
                self.w1_hi = sem(f"{n}_w1_hi")
                self.w1_lo = sem(f"{n}_w1_lo")
                self.w2_hi = sem(f"{n}_w2_hi")
                self.w2_lo = sem(f"{n}_w2_lo")
                self.half = sem(f"{n}_half")
                self.silu = sem(f"{n}_silu")
                self.u = sem(f"{n}_u")
                self.u_hi = sem(f"{n}_u_hi")
                self.u_lo = sem(f"{n}_u_lo")
                self.y_mm = sem(f"{n}_y_mm")
                self.y_add = sem(f"{n}_y_add")

        BOTH = [("post", 0), ("post", 1), ("pre", 0), ("post", 2), ("pre", 1), ("pre", 2)]
        n1 = Norms("n1", room0, CHUNKS, [("pre", 0), ("pre", 1), ("pre", 2)], None, 0, x_t, None)
        f1 = Ffn("f1", 0, room1, CHUNKS, n1)
        n2 = Norms("n2", room1, CHUNKS, BOTH, 0, 1, x_t, x1_d, overlapped=True)

        n3 = Norms("n3", room2, CHUNKS[:2], [("post", 0), ("post", 1), ("pre", 0), ("pre", 1)], 1, 2, x1_d, x2_d)
        f2 = Ffn("f2", 2, room2, CHUNKS[:2], n3)
        n4 = Norms("n4", room2, CHUNKS[:2], [("post", 0), ("post", 1)], 2, None, x2_d, out, overlapped=True)
        w_in_sem = [sem(f"w_in{i}") for i in range(2)]
        pj_hi, pj_lo, pj_mm, pj_out = (sem(f"pj_{n}") for n in ("hi", "lo", "mm", "out"))
        g_silu = sem("g_silu")
        z_mm, z_in, z_sp, z_cum = (sem(f"z_{n}") for n in ("mm", "in", "sp", "cum"))
        vt_mm, vt_out = sem("vt_mm"), sem("vt_out")
        kd_dif, kd_exp, kd_mul, kt_mm, kt_out, kv_mm, kv_add = (
            sem(f"g_{n}") for n in ("kd_dif", "kd_exp", "kd_mul", "kt_mm", "kt_out", "kv_mm", "kv_add"))
        lv_dif, lv_exp, lv_mul, lv_mm, lv_put, lv_base = (
            sem(f"lv_{n}") for n in ("dif", "exp", "mul", "mm", "put", "base"))
        qd_exp, qd_mul, o_mm, o_sq, o_out, o_stat, o_root, o_norm, o_hi, o_lo = (
            sem(f"go_{n}") for n in ("qd_exp", "qd_mul", "mm", "sq", "out", "stat", "root", "norm", "hi", "lo"))

        m_rope = sem("m_rope")
        m_w_in = [sem(f"m_w_in{i}") for i in range(2)]
        pr_sqd, pr_mm, pr_root, pr_mul, pr_hi, pr_lo, pr_rot, pr_khi, pr_klo = (
            sem(f"pr_{n}") for n in ("sqd", "mm", "root", "mul", "hi", "lo", "rot", "khi", "klo"))
        m_w_hi, m_w_lo, mk_mm, mk_hi, mk_lo, mq_mm, mq_raw, mq_rope, mq_hi, mq_lo, mv_mm, mv_hi, mv_lo = (
            sem(f"m_{n}") for n in ("w_hi", "w_lo", "k_mm", "k_hi", "k_lo", "q_mm", "q_raw", "q_rope", "q_hi", "q_lo",
                                    "v_mm", "v_hi", "v_lo"))
        mv_raw = sem("m_v_raw")
        c_mm, c_max, x_mm, x_row, s_mm, s_exp, pv_mm = (
            sem(f"m_{n}") for n in ("c_mm", "c_max", "x_mm", "x_row", "s_mm", "s_exp", "pv_mm"))
        part_hi = {"act": sem("m_p_hi_act"), "dve": sem("m_p_hi_dve")}
        part_lo = {"dve": sem("m_p_lo_dve"), "pool": sem("m_p_lo_pool")}
        acc_out, acc_root, acc_div, acc_hi, acc_lo = (sem(f"m_acc_{n}") for n in ("out", "root", "div", "hi", "lo"))
        wo_mm, wo_split_hi, wo_split_lo, wo_out, IN_TILES = sem("wo_mm"), pj_hi, pj_lo, pj_out, 16

        block = ctx.enter_context(nc.Block())

        def over_tiles(eng, tile, early=False):
            if not early:
                tile(0, 0, 0)
                tile(1, 1, 0)
            with eng.Fori(0, 3) as i:
                for slot in range(2):
                    tile(i * 2 + (2 + slot), slot, 0)
            with eng.Fori(0, 4) as i:
                for slot in range(2):
                    tile(i * 2 + (8 + slot), slot, 1)

        def proj_load(sp, t, slot, group=0):
            if not isinstance(t, int):
                sp.wait_ge(pj_lo, t - 1)
            sp.dma_start(wp_raw[:, slot], w_in[bass.ds(t, 1)].rearrange("a p k m -> p (a k) m"))\
                .then_inc(w_in_sem[slot], 16)

        def proj_high(act, t, slot):
            act.wait_ge(w_in_sem[slot], t * 8 + (16 - 8 * slot))
            if not isinstance(t, int) or t >= 2:
                act.wait_ge(pj_mm, t - 1)
            act.activation(wp_hi[:, slot], wp_raw[:, slot], ACT.Copy).then_inc(pj_hi, 1)

        def proj_low(dve, t, slot, group=0):
            dve.wait_ge(pj_hi, t + 1)
            dve.tensor_tensor(wp_lo[:, slot], wp_raw[:, slot], wp_hi[:, slot].bitcast(F32),
                              ALU.subtract).then_inc(pj_lo, 1)

        def first_two(step, eng):
            step(eng, 0, 0)
            step(eng, 1, 1)

        def proj_first_load(sp):
            sp.wait_ge(f1.y_mm, PAIRS * DK * len(CHUNKS))
            first_two(proj_load, sp)

        def proj_sync(sp):
            over_tiles(sp, lambda t, slot, group: proj_load(sp, t, slot), early=True)

        def proj_scalar(act):
            def split(t, slot, group):
                proj_high(act, t, slot)

            def leave(t, slot, group):
                tok = (TOK, LAT)[group]
                act.wait_ge(pj_mm, t + 1)
                src = bank[:, 3 * slot:3 * slot + 3].rearrange("p a b -> p (a b)")[:, 0:tok]
                dst = (proj_c, proj_l)[group][:, bass.ds(t - 8 * group, 1)].rearrange("p a b -> p (a b)")
                act.activation(dst, src, ACT.Copy).then_inc(pj_out, 1)

            act.wait_ge(n2.stored, 16 * len(CHUNKS))
            with act.Fori(0, 3) as i:
                for slot in range(2):
                    leave(i * 2 + slot, slot, 0)
                    split(i * 2 + (2 + slot), slot, 0)
            act.activation(pr_sq[:, :, :].rearrange("p a b -> p (a b)")[:, 0:TOK], kv_p, ACT.Square)\
                .then_inc(pr_sqd, 1)
            for slot in range(2):
                leave(6 + slot, slot, 0)
                split(8 + slot, slot, 1)
            act.wait_ge(pr_mm, 1)
            act.activation(pr_r[:, 0:LAT], bank[:, 6:8].rearrange("p a b -> p (a b)"), ACT.Ln, bias=eps[:, :],
                           scale=1.0 / KVRANK)
            link(act, "act", act.activation(pr_r[:, LAT:], bank[:, 2, 0:CTX], ACT.Ln, bias=eps[:, :],
                                            scale=1.0 / KVRANK))
            act.activation(pr_r[:, :], pr_r[:, :], ACT.Exp, scale=-0.5).then_inc(pr_root, 1)
            with act.Fori(0, 2) as i:
                for slot in range(2):
                    leave(i * 2 + (8 + slot), slot, 1)
                    split(i * 2 + (10 + slot), slot, 1)
            act.activation(pr_sq[:, :, :], qa_p, ACT.Square).then_inc(pr_sqd, 1)
            for slot in range(2):
                leave(12 + slot, slot, 1)
                split(14 + slot, slot, 1)
            act.wait_ge(pr_mm, 2)
            act.wait_ge(pr_mul, 1)
            r = pr_r[:, 0:LAT]
            link(act, "act", act.activation(r, bank[:, 6:8].rearrange("p a b -> p (a b)"), ACT.Ln, bias=eps[:, :],
                                            scale=1.0 / QRANK))
            act.activation(r, r, ACT.Exp, scale=-0.5).then_inc(pr_root, 1)
            leave(14, 0, 1)
            leave(15, 1, 1)

        def proj_vector(dve):
            def tiles(first, turns):
                with dve.Fori(0, turns) as i:
                    for slot in range(2):
                        proj_low(dve, i * 2 + (first + slot), slot)

            tiles(2, 3)
            proj_low(dve, 8, 0)
            proj_low(dve, 9, 1)
            dve.wait_ge(pr_root, 1)
            dve.scalar_tensor_tensor(out=kv_p, in0=kv_p, scalar=qk_norm_sb[:, 2:3], in1=pr_r[:, :], op0=ALU.mult,
                                     op1=ALU.mult).then_inc(pr_mul, 1)
            tiles(10, 2)
            proj_low(dve, 14, 0)
            proj_low(dve, 15, 1)
            dve.wait_ge(pr_root, 2)
            for k in range(2):
                last = dve.scalar_tensor_tensor(out=qa_p[:, k], in0=qa_p[:, k], scalar=qk_norm_sb[:, k:k + 1],
                                                in1=pr_r[:, 0:LAT], op0=ALU.mult, op1=ALU.mult)
            last.then_inc(pr_mul, 1)

        def proj_tensor(pe):
            def tile(t, slot, group):
                pe.wait_ge(pj_lo, t + 1)
                if not isinstance(t, int) or t >= 2:
                    pe.wait_ge(pj_out, t - 1)
                for c, (t0, w, _) in enumerate(CHUNKS[:3 - group]):
                    pe.wait_ge(n2.lo, DK * (c + 1))
                    acc = bank[:, 3 * slot + c, 0:w]
                    for k in range(DK):
                        hi, lo = room1.a_hi[:, k, t0:t0 + w], room1.a_lo[:, k, t0:t0 + w]
                        pe.matmul(acc, wp_hi[:, slot, k], hi, start=(k == 0), stop=False)
                        pe.matmul(acc, wp_hi[:, slot, k], lo, start=False, stop=False)
                        last = pe.matmul(acc, wp_lo[:, slot, k], hi, start=False, stop=(k == DK - 1))
                last.then_inc(pj_mm, 1)
            def tiles(first, turns, group):
                with pe.Fori(0, turns) as i:
                    for slot in range(2):
                        tile(i * 2 + (first + slot), slot, group)

            sq = pr_sq[:, :, :].rearrange("p a b -> p (a b)")
            tile(0, 0, 0)
            tile(1, 1, 0)
            tiles(2, 3, 0)
            pe.wait_ge(pr_sqd, 1)
            pe.wait_ge(pj_out, 7)
            for b, (t0, w, _) in zip((6, 7, 2), CHUNKS):
                last = pe.matmul(bank[:, b, 0:w], ones[:, :], sq[:, t0:t0 + w], start=True, stop=True)
            last.then_inc(pr_mm, 1)
            tiles(8, 3, 1)
            pe.wait_ge(pr_sqd, 2)
            pe.wait_ge(pr_root, 1)
            for c in range(2):
                for k in range(2):
                    last = pe.matmul(bank[:, 6 + c], ones[:, :], pr_sq[:, k, c * BANK:(c + 1) * BANK], start=(k == 0),
                                     stop=(k == 1))
            last.then_inc(pr_mm, 1)
            tile(14, 0, 1)
            tile(15, 1, 1)

        def halves(ap, s):
            return ap.rearrange("p (b h s) -> p b h s", h=2, s=s)

        def edge(ap, s, right):
            h = halves(ap, s)
            e = h[:, :, 1, 0:1] if right else h[:, :, 0, s - 1:s]
            return e.to_broadcast([P, LAT // (2 * s), s])

        LAST = (C - 1, 0)
        ORDER = ([8, 9] + list(range(8)), [9, 8] + list(range(7, -1, -1)))

        def gla_tensor(pe):
            pe.wait_ge(consts_in, CONSTS)
            pe.wait_ge(pj_out, 16)
            for i in range(4):
                if i >= 2:
                    pe.wait_ge(z_in, i - 1)
                for c, (t0, w, _) in enumerate(CHUNKS):
                    last = pe.matmul(bank[:, 3 * (i % 2) + c, 0:w], wa_sb[0:2 * GRANK, i],
                                     side_p[0:2 * GRANK, t0:t0 + w], start=True, stop=True)
                last.then_inc(z_mm, 1)
            for c in range(NC):
                if c >= 2:
                    pe.wait_ge(vt_out, c - 1)
                for h in range(GH):
                    last = pe.transpose(bank[:, 6 + c % 2, h * P:(h + 1) * P], gv_p[:, h, c * C:(c + 1) * C],
                                        ident[:, :])
                last.then_inc(vt_mm, 1)
            pe.wait_ge(z_in, 4)
            pe.wait_ge(vt_out, NC)
            for i in range(4):
                d, p = divmod(i, 2)
                pe.wait_ge(kd_mul, i + 1)
                if i:
                    pe.wait_ge(kt_out, i)
                for c in range(NC):
                    last = pe.transpose(bank[:, c // 4, c % 4 * C:(c % 4 + 1) * C],
                                        kd[:, i % 2, c * C:(c + 1) * C], ident[:, :])
                last.then_inc(kt_mm, 1)
                pe.wait_ge(kt_out, i + 1)
                if i:
                    pe.wait_ge(kv_add, 9 * i)
                for n, c in enumerate(ORDER[d][:-1]):
                    pe.matmul(bank[:, 3 + n // 2, n % 2 * 2 * GDV:(n % 2 + 1) * 2 * GDV], kd_tok[:, i % 2, c],
                              v_tok[:, c, 2 * p:2 * p + 2].rearrange("p a b -> p (a b)"), start=True,
                              stop=True).then_inc(kv_mm, 1)
            pe.wait_ge(kt_out, 4)
            pe.wait_ge(kv_add, 36)
            for n in range(2 * (LEVELS + 1)):
                level, p = divmod(n, 2)
                pe.wait_ge(lv_mul, n + 1)
                if n >= 2:
                    if n < 4:
                        pe.wait_ge(lv_base, n - 1)
                    else:
                        pe.wait_ge(lv_put, n - 3)
                k_of = gk_p[:, p] if level == LEVELS else k_lev[:, n % 2]
                for hh in range(2):
                    rows = slice(64 * hh, 64 * hh + 64)
                    for c in range(NC_LAT):
                        last = pe.matmul(bank[:, 4 * (n % 2) + 2 * hh + c // 4, c % 4 * C:(c % 4 + 1) * C],
                                         k_of[rows, c * C:(c + 1) * C], q_lev[rows, n % 2, c * C:(c + 1) * C],
                                         start=True, stop=True)
                last.then_inc(lv_mm, 1)
            pe.wait_ge(lv_put, 2 * LEVELS)
            pe.wait_ge(qd_mul, 4)
            def squares(n):
                pe.wait_ge(o_out, n + 1)
                pe.matmul(bank[:, n], ones[:, :], g_sq[:, n % 2], start=True, stop=True).then_inc(o_stat, 1)

            for n in range(2 * GH):
                h, quad = divmod(n, 2)
                p, rows = h // 2, slice(64 * (h % 2), 64 * (h % 2) + 64)
                for c in range(4 * quad, 4 * quad + 4):
                    acc = bank[:, n, c % 4 * C:(c % 4 + 1) * C]
                    pe.matmul(acc, v_tok[:, c, h], attn[:, h, c], start=True, stop=False)
                    for d in range(2):
                        last = pe.matmul(acc, state[rows, 2 * d + p, c], q_dec[rows, 2 * d + p, c * C:(c + 1) * C],
                                         start=False, stop=(d == 1))
                last.then_inc(o_mm, 1)
                if n:
                    squares(n - 1)
            squares(2 * GH - 1)

        def gla_scalar(act):
            act.wait_ge(pj_out, 16)
            act.activation(gg_p.rearrange("p a b -> p (a b)"), gg_p.rearrange("p a b -> p (a b)"), ACT.Silu)\
                .then_inc(g_silu, 1)
            act.preload_act_table_set(EXP_LN)
            for i in range(4):
                act.wait_ge(z_in, i + 1)
                t = zl[:, i % 2]
                link(act, "act", act.activation(t, z[:, i % 2], ACT.Abs))
                link(act, "act", act.activation(t, t, ACT.Exp, scale=-1.0))
                act.activation(t, t, ACT.Ln, bias=1.0).then_inc(z_sp, 1)
            for c in range(NC):
                act.wait_ge(vt_mm, c + 1)
                act.activation(v_tok[:, c].rearrange("p a b -> p (a b)"), bank[:, 6 + c % 2], ACT.Copy)\
                    .then_inc(vt_out, 1)
            for i in range(4):
                d = i // 2
                act.wait_ge(kd_dif, i + 1)
                act.activation(kd[:, i % 2], kd[:, i % 2], ACT.Exp, scale=1 / GATE_NORM).then_inc(kd_exp, 1)
                last = cum[:, i].rearrange("p (c t) -> p c t", t=C)[:, :, LAST[d]]
                act.activation(decay[:, i], last, ACT.Exp, scale=1 / GATE_NORM).then_inc(kd_exp, 1)
                act.wait_ge(kt_mm, i + 1)
                src = bank[:, 0:3].rearrange("p a b -> p (a b)")[:, 0:TOK]
                if i >= 2:
                    act.wait_ge(kv_mm, 9 * (i - 1))
                act.activation(kd_tok[:, i % 2].rearrange("p a b -> p (a b)"), src, ACT.Copy).then_inc(kt_out, 1)
            for n in range(2 * LEVELS):
                act.wait_ge(lv_dif, n + 1)
                t = diff[:, n % 2].rearrange("p a b -> p (a b)")
                act.activation(t, t, ACT.Exp, scale=1 / GATE_NORM).then_inc(lv_exp, 1)
                if n in (2, 3):
                    act.wait_ge(lv_mm, n - 1)
                    act.activation(attn[:, 2 * (n - 2):2 * (n - 2) + 2].rearrange("p a b c -> p (a b c)"),
                                   bank[:, 4 * (n - 2):4 * (n - 2) + 4].rearrange("p a b -> p (a b)"), ACT.Copy)\
                        .then_inc(lv_base, 1)
            act.wait_ge(lv_mm, 2 * (LEVELS + 1))
            for i in range(4):
                act.activation(q_dec[:, i], cum[:, i, 0:LAT], ACT.Exp, scale=1 / GATE_NORM).then_inc(qd_exp, 1)
            for n in range(2 * GH):
                h, quad = divmod(n, 2)
                act.wait_ge(o_mm, n + 1)
                if n >= 2:
                    act.wait_ge(o_stat, n - 1)
                act.activation(g_sq[:, n % 2], bank[:, n], ACT.Square, scale=GDK ** -0.5).then_inc(o_sq, 1)
                act.activation(o_gla[:, h, quad * BANK:(quad + 1) * BANK], bank[:, n], ACT.Copy,
                               scale=GDK ** -0.5).then_inc(o_out, 1)
                if n >= 2:
                    root(act, n - 2)
                if n >= 3:
                    gla_high(act, n - 3)
            act.activation(kvn_hi[:, :], kv_p, ACT.Copy).then_inc(pr_hi, 1)
            for n in (2 * GH - 2, 2 * GH - 1):
                root(act, n)
                gla_high(act, n - 1)
            gla_high(act, 2 * GH - 1)

        def gla_high(act, n):
            h, t0 = n // 2, n % 2 * BANK
            act.wait_ge(o_norm, n + 1)
            act.activation(mix_hi[:, GH + h, t0:t0 + BANK], o_gla[:, h, t0:t0 + BANK], ACT.Copy).then_inc(o_hi, 1)

        def root(act, n):
            act.wait_ge(o_stat, n + 1)
            if n >= 2:
                act.wait_ge(o_norm, n - 1)
            r = g_rstd[:, n % 2]
            link(act, "act", act.activation(r, bank[:, n], ACT.Ln, bias=eps[:, :], scale=1.0 / GDV))
            act.activation(r, r, ACT.Exp, scale=-0.5).then_inc(o_root, 1)

        def gla_vector(dve):
            dve.wait_ge(filled, SCAN_FILLS)
            for i in range(4):
                dve.wait_ge(z_mm, i + 1)
                if i >= 2:
                    dve.wait_ge(z_cum, 2 * (i - 1))
                src = bank[:, 3 * (i % 2):3 * (i % 2) + 3].rearrange("p a b -> p (a b)")[:, 0:TOK]
                dve.tensor_scalar(z[:, i % 2], src, ba_sb[:, i:i + 1], None, ALU.add).then_inc(z_in, 1)
                if i:
                    gla_sum(dve, i - 1)
            gla_sum(dve, 3)
            dve.wait_ge(z_cum, 8)
            dve.wait_ge(z_sp, 4)
            for i in range(4):
                d, p = divmod(i, 2)
                v = cum[:, i].rearrange("p (c t) -> p c t", t=C)
                if i >= 2:
                    dve.wait_ge(kt_mm, i - 1)
                t = kd[:, i % 2].rearrange("p (c t) -> p c t", t=C)
                dve.tensor_tensor(t, v[:, :, LAST[d]:LAST[d] + 1].to_broadcast([P, NC, C]), v, ALU.subtract)\
                    .then_inc(kd_dif, 1)
                dve.wait_ge(kd_exp, 2 * i + 2)
                dve.tensor_tensor(kd[:, i % 2], kd[:, i % 2], gk_p[:, p], ALU.mult).then_inc(kd_mul, 1)
                if i:
                    gla_chain(dve, i - 1)
            gla_chain(dve, 3)
            for n in range(2 * (LEVELS + 1)):
                level, p = divmod(n, 2)
                s = C // 2 >> level
                if n >= 2:
                    dve.wait_ge(lv_mul, n - 1)
                else:
                    dve.wait_ge(kt_mm, 4)
                    dve.wait_ge(kv_mm, 36)
                if level < LEVELS:
                    for d in range(2):
                        v, t = halves(cum[:, 2 * d + p, 0:LAT], s), halves(diff[:, n % 2, d], s)
                        e = edge(cum[:, 2 * d + p, 0:LAT], s, right=bool(d))
                        far = 1 - d
                        dve.tensor_tensor(t[:, :, far], v[:, :, far], e, ALU.subtract)
                        last = dve.tensor_tensor(t[:, :, 1 - far], e, v[:, :, 1 - far], ALU.subtract)
                    last.then_inc(lv_dif, 1)
                else:
                    dve.wait_ge(lv_mul, n)
                    dve.wait_ge(lv_mm, n - 1)
                    dve.tensor_scalar(q_lev[:, n % 2], gq_p[:, p], 2.0, None, ALU.mult).then_inc(lv_mul, 1)
                if n >= 4:
                    gla_put(dve, n - 2)
            gla_put(dve, 2 * LEVELS)
            gla_put(dve, 2 * LEVELS + 1)
            for i in range(4):
                dve.wait_ge(qd_exp, i + 1)
                dve.tensor_tensor(q_dec[:, i], q_dec[:, i], gq_p[:, i % 2], ALU.mult).then_inc(qd_mul, 1)
            dve.wait_ge(g_silu, 1)
            for n in range(2 * GH):
                h, quad = divmod(n, 2)
                t0 = quad * BANK
                dve.wait_ge(o_root, n + 1)
                o = o_gla[:, h, t0:t0 + BANK]
                link(dve, "dve", dve.scalar_tensor_tensor(out=o, in0=o, scalar=gnorm_sb[:, 0:1], in1=g_rstd[:, n % 2],
                                                          op0=ALU.mult, op1=ALU.mult))
                dve.tensor_tensor(o, o, gg_p[:, h, t0:t0 + BANK], ALU.mult).then_inc(o_norm, 1)

        def gla_low(dve, n):
            h, t0 = n // 2, n % 2 * BANK
            dve.wait_ge(o_mm, 2 * GH)
            dve.wait_ge(o_hi, n + 1)
            dve.tensor_tensor(mix_lo[:, GH + h, t0:t0 + BANK], o_gla[:, h, t0:t0 + BANK],
                              mix_hi[:, GH + h, t0:t0 + BANK].bitcast(F32), ALU.subtract).then_inc(o_lo, 1)

        def gla_sum(dve, i):
            dve.wait_ge(z_sp, i + 1)
            t = zl[:, i % 2]
            dve.scalar_tensor_tensor(out=t, in0=z[:, i % 2], scalar=0.0, in1=t, op0=ALU.min,
                                     op1=ALU.subtract).then_inc(z_cum, 1)
            dve.wait_ge(z_cum, 2 * i + 1)
            if i < 2:
                dve.tensor_tensor_scan(cum[:, i], keep[:, 0:TOK], t, 0.0, ALU.mult, ALU.add).then_inc(z_cum, 1)
            else:
                dve.tensor_tensor_scan(cum[:, i, ::-1], keep[:, 1:TOK + 1][:, ::-1], t[:, ::-1], 0.0, ALU.mult,
                                       ALU.add).then_inc(z_cum, 1)

        def gla_chain(dve, i):
            d = i // 2
            for n, c in enumerate(ORDER[d][:-1]):
                dve.wait_ge(kv_mm, 9 * i + min(NC - 1, n // 2 * 2 + 2))
                if n:
                    dve.wait_ge(kv_add, 9 * i + n)
                after = ORDER[d][n + 1]
                for hh in range(2):
                    rows = slice(64 * hh, 64 * hh + 64)
                    kv = bank[rows, 3 + n // 2, (n % 2 * 2 + hh) * GDV:(n % 2 * 2 + hh + 1) * GDV]
                    if n:
                        last = dve.scalar_tensor_tensor(out=state[rows, i, after], in0=state[rows, i, c],
                                                        scalar=decay[rows, i, c:c + 1], in1=kv, op0=ALU.mult,
                                                        op1=ALU.add)
                    else:
                        last = dve.tensor_copy(state[rows, i, after], kv)
                last.then_inc(kv_add, 1)

        def gla_put(dve, n):
            level, p = divmod(n, 2)
            dve.wait_ge(lv_mm, n + 1)
            dve.wait_ge(lv_base, 2)
            if n >= 4:
                dve.wait_ge(lv_put, n - 3)
            for hh in range(2):
                for quad in range(2):
                    last = dve.copy_predicated(attn[:, 2 * p + hh, 4 * quad:4 * quad + 4].rearrange("p a b -> p (a b)"),
                                               mask[:, level - 1], bank[:, 4 * (n % 2) + 2 * hh + quad])
            last.then_inc(lv_put, 1)

        def gla_pool(pool):
            pool.wait_ge(pj_mm, 16)
            pool.memset(keep[:, :], 1.0).then_inc(filled, 1)
            pool.wait_ge(filled, SCAN_FILLS - 1)
            for c in range(NC + 1):
                last = pool.memset(keep[:, c * C:c * C + 1], 0.0)
            last.then_inc(filled, 1)
            for n in range(2 * LEVELS):
                level, p = divmod(n, 2)
                s = C // 2 >> level
                pool.wait_ge(lv_exp, n + 1)
                if n >= 2:
                    pool.wait_ge(lv_mm, n - 1)
                f, b = halves(diff[:, n % 2, 0], s), halves(diff[:, n % 2, 1], s)
                q, k = halves(gq_p[:, p], s), halves(gk_p[:, p, 0:LAT], s)
                ql, kl = halves(q_lev[:, n % 2], s), halves(k_lev[:, n % 2], s)
                pool.tensor_tensor(ql[:, :, 1], q[:, :, 1], f[:, :, 1], ALU.mult)
                pool.tensor_tensor(ql[:, :, 0], q[:, :, 0], b[:, :, 0], ALU.mult)
                pool.tensor_tensor(kl[:, :, 0], k[:, :, 0], f[:, :, 0], ALU.mult)
                pool.tensor_tensor(kl[:, :, 1], k[:, :, 1], b[:, :, 1], ALU.mult).then_inc(lv_mul, 1)


        PAIRS = FJ // 2

        def over_hidden(eng, prologue, pair, tail):
            prologue()
            with eng.Fori(0, (PAIRS - 1) // 2) as i:
                for k in range(2):
                    pair(i * 2 + (k + 1), 2 if k == 0 else 0)
            tail()

        def w1_load(sp, f, j, half):
            if not isinstance(j, int) or j >= 1:
                sp.wait_ge(f.w1_lo, j * 2 + (half - 1))
            sp.dma_start(f.room.w1_raw[:, half], f.w_in[bass.ds(j * 2 + half, 1)].rearrange("a p k m -> p (a k) m"))\
                .then_inc(f.w1_in[half], 16)

        def first_load(sp, f):
            w1_load(sp, f, 0, 0)
            w1_load(sp, f, 0, 1)

        def ffn_sync(sp, f, more=lambda k: None, early=False):
            def load_half(j, half):
                w1_load(sp, f, j, half)

            def load_w2(j):
                if not isinstance(j, int) or j >= 1:
                    sp.wait_ge(f.w2_lo, j)
                sp.dma_start(f.room.w2_raw[:, :], f.w_out[bass.ds(j, 1)].rearrange("a p m -> p (a m)")).then_inc(f.w2_in, 16)

            if not early:
                first_load(sp, f)
            load_half(1, 0)
            load_half(1, 1)
            load_w2(0)
            more(0)
            load_half(2, 0)
            more(1)
            load_half(2, 1)
            more(2)
            load_w2(1)
            with sp.Fori(0, FJ - 3) as i:
                load_half(i + 3, 0)
                load_half(i + 3, 1)
                load_w2(i + 2)
            load_w2(FJ - 1)

        def ffn_tensor(pe, f, behind):
            nch = len(f.chunks)

            def hidden(j):
                for half in range(2):
                    pe.wait_ge(f.w1_lo, j * 2 + (half + 1))
                    if not isinstance(j, int) or j >= 1:
                        pe.wait_ge(f.silu if half == 0 else f.u, j)
                    for c, (t0, w, _) in enumerate(f.chunks):
                        pe.wait_ge(f.norms.lo, DK * (c + 1))
                        acc = bank[:, 3 * half + c, 0:w]
                        for k in range(DK):
                            hi, lo = f.room.a_hi[:, k, t0:t0 + w], f.room.a_lo[:, k, t0:t0 + w]
                            pe.matmul(acc, f.room.w1_hi[:, half, k], hi, start=(k == 0), stop=False)
                            pe.matmul(acc, f.room.w1_hi[:, half, k], lo, start=False, stop=False)
                            last = pe.matmul(acc, f.room.w1_lo[:, half, k], hi, start=False, stop=(k == DK - 1))
                    last.then_inc(f.half, 1)

            def project(g, even, closing=False):
                pe.wait_ge(f.u_lo, g * 2 + 2)
                pe.wait_ge(f.w2_lo, g * 2 + 2)
                for c, (t0, w, _) in enumerate(f.chunks):
                    for m in range(DK):
                        n = c * DK + m
                        if closing and n == DK + DK // 2:
                            norm_step(pe, behind, 0)
                        pe.wait_ge(f.y_add, g * (DK * nch) + (n + 1))
                        acc = bank[:, 6 + n % 2, 0:w]
                        for i, slot in enumerate((even, 1)):
                            hi, lo = f.room.u_hi[:, slot, t0:t0 + w], f.room.u_lo[:, slot, t0:t0 + w]
                            w_hi, w_lo = f.room.w2_hi[:, i, m * P:(m + 1) * P], f.room.w2_lo[:, i, m * P:(m + 1) * P]
                            pe.matmul(acc, w_hi, hi, start=(i == 0), stop=False)
                            pe.matmul(acc, w_hi, lo, start=False, stop=False)
                            last = pe.matmul(acc, w_lo, hi, start=False, stop=(i == 1))
                        last.then_inc(f.y_mm, 1)

            def prologue():
                hidden(0)
                hidden(1)

            def pair(g, even):
                hidden(g * 2)
                project(g - 1, 2 - even)
                hidden(g * 2 + 1)

            over_hidden(pe, prologue, pair, lambda: project(PAIRS - 1, 0, closing=True))

        def w1_part_high(act, f, j, half):
            act.wait_ge(f.w1_in[half], (j + 1) * 16)
            if not isinstance(j, int) or j >= 1:
                act.wait_ge(f.half, j * 2 + (half - 1))
            act.activation(f.room.w1_hi[:, half], f.room.w1_raw[:, half], ACT.Copy).then_inc(f.w1_hi, 1)

        def w1_part_low(dve, f, j, half):
            dve.wait_ge(f.w1_hi, j * 2 + (half + 1))
            dve.tensor_tensor(f.room.w1_lo[:, half], f.room.w1_raw[:, half], f.room.w1_hi[:, half].bitcast(F32),
                              ALU.subtract).then_inc(f.w1_lo, 1)

        def first_high(act, f):
            w1_part_high(act, f, 0, 0)
            w1_part_high(act, f, 0, 1)

        def first_low(dve, f):
            w1_part_low(dve, f, 0, 0)
            w1_part_low(dve, f, 0, 1)

        def ffn_scalar(act, f, more=lambda: None, early=False):
            nch = len(f.chunks)

            def w1_high(j, half):
                w1_part_high(act, f, j, half)

            def w2_high(j, slot):
                act.wait_ge(f.w2_in, (j + 1) * 16)
                if not isinstance(j, int) or j >= 2:
                    act.wait_ge(f.y_mm, (j - slot) * (DK * nch // 2))
                act.activation(f.room.w2_hi[:, slot], f.room.w2_raw[:, :], ACT.Copy).then_inc(f.w2_hi, 1)

            def silu(j):
                act.wait_ge(f.half, j * 2 + 1)
                if not isinstance(j, int) or j >= 1:
                    act.wait_ge(f.u_lo, j)
                gate = bank[:, 0:3].rearrange("p a b -> p (a b)")[:, 0:f.tok]
                act.activation(f.room.u_f[:, 0:f.tok], gate, ACT.Silu).then_inc(f.silu, 1)

            def u_high(j, slot):
                act.wait_ge(f.u, j + 1)
                act.activation(f.room.u_hi[:, slot, 0:f.tok], f.room.u_f[:, 0:f.tok], ACT.Copy).then_inc(f.u_hi, 1)

            def prologue():
                if not early:
                    first_high(act, f)
                more()
                w1_high(1, 0)
                silu(0)
                w1_high(1, 1)
                u_high(0, 0)
                w2_high(0, 0)
                w1_high(2, 0)
                silu(1)
                w1_high(2, 1)
                u_high(1, 1)
                w2_high(1, 1)

            def pair(g, even, last=False):
                w1_high(g * 2 + 1, 0)
                silu(g * 2)
                w1_high(g * 2 + 1, 1)
                u_high(g * 2, even)
                w2_high(g * 2, 0)
                if not last:
                    w1_high(g * 2 + 2, 0)
                silu(g * 2 + 1)
                if not last:
                    w1_high(g * 2 + 2, 1)
                u_high(g * 2 + 1, 1)
                w2_high(g * 2 + 1, 1)

            act.preload_act_table_set("silu_and_others")
            prologue()
            with act.Fori(0, (PAIRS - 3) // 2) as i:
                pair(i * 2 + 1, 2)
                pair(i * 2 + 2, 0)
            pair(PAIRS - 2, 2)
            pair(PAIRS - 1, 0, last=True)

        def ffn_vector(dve, f, more=lambda k: None, early=False):
            nch = len(f.chunks)

            def w1_low(j, half):
                w1_part_low(dve, f, j, half)

            def w2_low(j, slot):
                dve.wait_ge(f.w2_hi, j + 1)
                dve.tensor_tensor(f.room.w2_lo[:, slot], f.room.w2_raw[:, :], f.room.w2_hi[:, slot].bitcast(F32),
                                  ALU.subtract).then_inc(f.w2_lo, 1)

            def gated(j):
                dve.wait_ge(f.half, j * 2 + 2)
                dve.wait_ge(f.silu, j + 1)
                value = bank[:, 3:6].rearrange("p a b -> p (a b)")[:, 0:f.tok]
                dve.tensor_tensor(f.room.u_f[:, 0:f.tok], f.room.u_f[:, 0:f.tok], value, ALU.mult).then_inc(f.u, 1)

            def u_low(j, slot):
                dve.wait_ge(f.u_hi, j + 1)
                dve.tensor_tensor(f.room.u_lo[:, slot, 0:f.tok], f.room.u_f[:, 0:f.tok], f.room.u_hi[:, slot, 0:f.tok].bitcast(F32),
                                  ALU.subtract).then_inc(f.u_lo, 1)

            def add(g, c, m):
                t0, w, _ = f.chunks[c]
                n = c * DK + m
                dve.wait_ge(f.y_mm, g * (DK * nch) + (n + 1))
                y = f.room.res[:, m, t0:t0 + w]
                dve.tensor_tensor(y, y, bank[:, 6 + n % 2, 0:w], ALU.add).then_inc(f.y_add, 1)

            def prologue():
                if not early:
                    first_low(dve, f)
                w1_low(1, 0)
                more(6)
                gated(0)
                more(3)
                w1_low(1, 1)
                u_low(0, 0)
                more(3)
                w2_low(0, 0)
                more(3)
                w1_low(2, 0)
                more(3)
                gated(1)
                more(3)
                w1_low(2, 1)
                u_low(1, 1)
                more(3)
                w2_low(1, 1)

            def pair(g, even, last=False):
                w1_low(g * 2 + 1, 0)
                for n in range(DK * nch):
                    add(g - 1, n // DK, n % DK)
                    if n == 3:
                        gated(g * 2)
                    if n == 6:
                        w1_low(g * 2 + 1, 1)
                    if n == 9:
                        u_low(g * 2, even)
                w2_low(g * 2, 0)
                if not last:
                    w1_low(g * 2 + 2, 0)
                gated(g * 2 + 1)
                if not last:
                    w1_low(g * 2 + 2, 1)
                u_low(g * 2 + 1, 1)
                w2_low(g * 2 + 1, 1)

            prologue()
            dve.wait_ge(f.y_add, 2)
            with dve.Fori(0, (PAIRS - 3) // 2) as i:
                pair(i * 2 + 1, 2)
                pair(i * 2 + 2, 0)
            pair(PAIRS - 2, 2)
            pair(PAIRS - 1, 0, last=True)
            for n in range(DK * nch):
                add(PAIRS - 1, n // DK, n % DK)

        SCALE = QK ** -0.5
        UNITS = 2 * NC
        QT = LAT // P
        AHEAD = 3
        KEYS, QUERIES, Q_PARTS, VALUES = 0, 2, 3, 4
        TURN = 16
        HI_ON = ["act" if n % 2 == 0 else "dve" for n in range(UNITS)]
        LO_ON = ["dve" if n % 3 == 1 else "pool" for n in range(UNITS)]
        COARSE = dict(zip((5, 6, 8, 9, 11, 12, 14, 15), range(QT)))
        NUM = (slice(0, 64), slice(64, 128))
        DEN = (slice(64, 128), slice(0, 64))
        VCOL = (0, 64)

        def coarse_bank(h, t):
            return 3 * (t % 2) if is_first(h) else 0

        def is_first(h):
            return isinstance(h, int) and h == 0

        def split_done(eng, sems, on, h, n):
            who = on[n]
            eng.wait_ge(sems[who], h * on.count(who) + on[:n + 1].count(who))

        def over_heads(eng, first, body):
            first()
            with eng.Fori(0, HEADS // 2 - 1) as i:
                for slot in range(2):
                    body(i * 2 + slot, slot, False)
            body(HEADS - 2, 0, False)
            body(HEADS - 1, 1, True)

        def after(h, slot, n):
            return (h, slot, n + AHEAD) if n + AHEAD < UNITS else (h + 1, 1 - slot, n + AHEAD - UNITS)

        def mla_sync(sp):
            sp.wait_ge(o_mm, 2 * GH)
            sp.dma_start(rope[NOPE:], rope_d[NOPE:]).then_inc(m_rope, 16)

            def load(h, slot):
                sp.dma_start(wq_raw[:, slot], w_qb[bass.ds(h, 1)].rearrange("a p k m -> p (a k) m"))\
                    .then_inc(m_w_in[slot], 16)
                sp.dma_start(wkv_raw[:, slot], w_kvb[bass.ds(h, 1)].rearrange("a p m -> p (a m)"))\
                    .then_inc(m_w_in[slot], 16)

            load(0, 0)
            load(1, 1)
            with sp.Fori(0, HEADS // 2 - 1) as i:
                for slot in range(2):
                    h = i * 2 + slot
                    sp.wait_ge(m_w_lo, h * 2 + 2)
                    load(h + 2, slot)

        def mla_pool(pool):
            pool.wait_ge(o_norm, 2 * GH)
            pool.memset(k_hi[QK:QK + 1, :, :].bitcast(F32), 1.0).then_inc(filled, 1)
            pool.memset(k_lo[QK:QK + 1, :, :].bitcast(F32), 0.0).then_inc(filled, 1)
            pool.memset(q_lo[QK:QK + 1, :, :].bitcast(F32), 0.0).then_inc(filled, 1)
            pool.wait_ge(filled, SCAN_FILLS + 3)
            pool.wait_ge(pr_klo, 2)
            pool.memset(row_max[:, :, :], 0.0).then_inc(filled, 1)
            pool.memset(acc_f[:, :], 0.0).then_inc(acc_lo, 1)
            pool.memset(acc_r[:, :], 0.0).then_inc(acc_out, 1)
            for slot in range(2):
                cols = slice(64 - VCOL[slot], 128 - VCOL[slot])
                pool.memset(v_hi[:, slot, :, cols].bitcast(F32), 1.0).then_inc(filled, 1)
                pool.memset(v_lo[:, slot, :, cols].bitcast(F32), 0.0).then_inc(filled, 1)

            def first():
                for n in range(AHEAD):
                    low(pool, "pool", 0, n)

            def body(h, slot, last):
                for n in range(UNITS):
                    g, _, m = after(h, slot, n)
                    if not (last and n + AHEAD >= UNITS):
                        low(pool, "pool", g, m)

            over_heads(pool, first, body)

        def low(eng, who, h, n):
            if LO_ON[n] == who:
                split_done(eng, part_hi, HI_ON, h, n)
                eng.tensor_tensor(p_lo[:, n % 4], p_f[:, n % 4], p_hi[:, n % 4].bitcast(F32), ALU.subtract)\
                    .then_inc(part_lo[who], 1)

        def mla_tensor(pe):
            def three(acc, w_hi, w_lo, x_hi, x_lo, start=True, stop=True):
                pe.matmul(acc, w_hi, x_hi, start=start, stop=False)
                pe.matmul(acc, w_hi, x_lo, start=False, stop=False)
                return pe.matmul(acc, w_lo, x_hi, start=False, stop=stop)

            def keys(h, slot):
                pe.wait_ge(m_w_lo, h * 2 + 2)
                pe.wait_ge(x_row, h)
                for c, (t0, w, _) in enumerate(CHUNKS):
                    last = three(bank[:, c, 0:w], wkv_hi[:, slot], wkv_lo[:, slot], kvn_hi[:, t0:t0 + w],
                                 kvn_lo[:, t0:t0 + w])
                last.then_inc(mk_mm, 1)

            def queries(h, slot):
                pe.wait_ge(mk_lo, h + 1)
                pe.wait_ge(mv_raw, h * 2 + 2)
                for c in range(2):
                    for k in range(2):
                        x = slice(c * BANK, (c + 1) * BANK)
                        last = three(bank[:, c], wq_hi[:, slot, k], wq_lo[:, slot, k], qn_hi[:, k, x], qn_lo[:, k, x],
                                     k == 0, k == 1)
                last.then_inc(mq_mm, 1)

            def queries_read(h):
                pe.wait_ge(mq_rope, h * 3 + 3)
                pe.wait_ge(mq_raw, h + 1)

            def values(h, slot):
                acc = bank[:, 0:2].rearrange("p a b -> p (a b)")
                for t in range(NC):
                    src = vt_lat[:, t * C:(t + 1) * C] if t < NC_LAT else vt_ctx[0:VD, (t - NC_LAT) * C:(t - NC_LAT + 1) * C]
                    last = pe.transpose(acc[:, t * VD:(t + 1) * VD], src, ident[0:VD, 0:VD])
                last.then_inc(mv_mm, 1)

            def coarse(h, slot, t):
                if t == 0:
                    pe.wait_ge(mq_hi, h + 1)
                    pe.wait_ge(mv_lo, h + 1)
                at = coarse_bank(h, t)
                if is_first(h):
                    if t >= 2:
                        pe.wait_ge(c_max, t - 1)
                else:
                    pe.wait_ge(c_max, h * QT + t)
                for c, (t0, w, _) in enumerate(CHUNKS):
                    last = pe.matmul(bank[:, at + c, 0:w], q_hi[0:QK, slot, t * P:(t + 1) * P],
                                     k_hi[0:QK, slot, t0:t0 + w], start=True, stop=True)
                last.then_inc(c_mm, 1)

            def turn(h):
                pe.wait_ge(c_max, h * QT + QT)
                for t in range(QT):
                    last = pe.transpose(bank[0:QK + 1, t // 4, t % 4 * P:(t % 4 + 1) * P], row_max[:, t], ident[:, :])
                last.then_inc(x_mm, 1)

            def prepare(h, slot, n):
                if n == KEYS:
                    keys(h, slot)
                if n == QUERIES:
                    queries(h, slot)
                if n == VALUES:
                    values(h, slot)
                if n in COARSE:
                    coarse(h, slot, COARSE[n])
                if n == TURN:
                    turn(h)

            def scores(h, slot, n):
                if n == KEYS:
                    for s in (mk_lo, mq_lo, x_row):
                        pe.wait_ge(s, h + 1)
                half, t = divmod(n, NC)
                x = slice(half * BANK, (half + 1) * BANK)
                t = slice(t * C, (t + 1) * C)
                three(bank[:, 3 + n % 4], k_hi[0:QK + 1, slot, t], k_lo[0:QK + 1, slot, t], q_hi[0:QK + 1, slot, x],
                      q_lo[0:QK + 1, slot, x]).then_inc(s_mm, 1)

            def product(h, slot, n):
                half, t = divmod(n, NC)
                split_done(pe, part_lo, LO_ON, h, n)
                if t == 0:
                    pe.wait_ge(acc_out, h * 2 + half + 1)
                three(bank[:, 7], v_hi[:, slot, t], v_lo[:, slot, t], p_hi[:, n % 4], p_lo[:, n % 4], t == 0,
                      t == NC - 1).then_inc(pv_mm, 1)

            def first():
                pe.wait_ge(pr_lo, 1)
                for n in range(TURN + 1):
                    if n == QUERIES:
                        pe.wait_ge(pr_lo, 2)
                    if n == VALUES:
                        queries_read(0)
                        pe.wait_ge(filled, MLA_FILLS)
                    prepare(0, 0, n)
                for n in range(AHEAD):
                    scores(0, 0, n)

            def body(h, slot, last):
                for n in range(UNITS):
                    if not (last and n + AHEAD >= UNITS):
                        scores(*after(h, slot, n))
                    if n == VALUES and not last:
                        queries_read(h + 1)
                    product(h, slot, n)
                    if not last:
                        prepare(h + 1, 1 - slot, n)

            over_heads(pe, first, body)

        def mla_scalar(act):
            def split(h, slot):
                act.wait_ge(m_w_in[slot], h * 16 + (32 - 16 * slot))
                if not isinstance(h, int):
                    act.wait_ge(mv_mm, h - 1)
                act.activation(wq_hi[:, slot], wq_raw[:, slot], ACT.Copy).then_inc(m_w_hi, 1)
                act.activation(wkv_hi[:, slot], wkv_raw[:, slot], ACT.Copy).then_inc(m_w_hi, 1)

            split(0, 0)
            split(1, 1)
            act.wait_ge(pr_rot, 4)
            for slot in range(2):
                act.activation(k_hi[NOPE:QK, slot], k_f[NOPE:QK], ACT.Copy).then_inc(pr_khi, 1)
            act.activation(qn_hi[:, :, :], qa_p, ACT.Copy).then_inc(pr_hi, 1)

            def prepare(h, slot, n):
                if n == KEYS:
                    act.wait_ge(mk_mm, h + 1)
                    act.activation(k_hi[0:NOPE, slot], bank[0:NOPE, 0:3].rearrange("p a b -> p (a b)")[:, 0:TOK],
                                   ACT.Copy).then_inc(mk_hi, 1)
                    act.wait_ge(mv_mm, h)
                    act.activation(vt_lat, bank[NOPE:, 0:2].rearrange("p a b -> p (a b)"), ACT.Copy).then_inc(mv_raw, 1)
                    act.activation(vt_ctx[0:VD], bank[NOPE:, 2, 0:CTX], ACT.Copy).then_inc(mv_raw, 1)
                if n == QUERIES:
                    act.wait_ge(mq_mm, h + 1)
                    act.wait_ge(mq_lo, h)
                    act.activation(q_f[0:NOPE], bank[0:NOPE, 0:2].rearrange("p a b -> p (a b)"), ACT.Copy)\
                        .then_inc(mq_raw, 1)
                if n == Q_PARTS:
                    act.wait_ge(mq_rope, h * 3 + 3)
                    act.wait_ge(mq_raw, h + 1)
                    act.activation(q_hi[0:QK, slot], q_f[0:QK], ACT.Copy).then_inc(mq_hi, 1)
                if n == VALUES:
                    act.wait_ge(mv_mm, h + 1)
                    src = bank[:, 0:2].rearrange("p a b -> p (a b)")[:, 0:NC * VD].rearrange("p (t v) -> p t v", v=VD)
                    act.activation(v_hi[:, slot, :, VCOL[slot]:VCOL[slot] + VD], src, ACT.Copy).then_inc(mv_hi, 1)
                if n == TURN:
                    act.wait_ge(x_mm, h + 1)
                    act.activation(q_hi[QK:QK + 1, slot], bank[QK:QK + 1, 0:2].rearrange("p a b -> p (a b)"),
                                   ACT.Copy, scale=-1.0).then_inc(x_row, 1)

            def exps(h, n):
                act.wait_ge(s_mm, h * UNITS + (n + 1))
                act.activation(p_f[:, n % 4], bank[:, 3 + n % 4], ACT.Exp, scale=SCALE).then_inc(s_exp, 1)
                if HI_ON[n] == "act":
                    act.wait_ge(s_exp, h * UNITS + (n + 1))
                    act.activation(p_hi[:, n % 4], p_f[:, n % 4], ACT.Copy).then_inc(part_hi["act"], 1)

            def finish(h, slot, half):
                a = h * 2 + half
                act.wait_ge(acc_out, a + 2)
                act.activation(acc_r[NUM[slot]], acc_f[DEN[slot]], ACT.Ln).then_inc(acc_root, 1)
                act.wait_ge(acc_root, a * 2 + 1)
                act.activation(acc_r[NUM[slot]], acc_r[NUM[slot]], ACT.Exp, scale=-1.0).then_inc(acc_root, 1)
                act.wait_ge(acc_div, a + 1)
                act.activation(mixed(mix_hi, h, slot, half), acc_f[NUM[slot]], ACT.Copy).then_inc(acc_hi, 1)

            def first():
                for n in range(TURN + 1):
                    prepare(0, 0, n)
                act.wait_ge(o_lo, 2 * GH)
                for n in range(AHEAD):
                    exps(0, n)

            def body(h, slot, last):
                for n in range(UNITS):
                    g, _, m = after(h, slot, n)
                    if not (last and n + AHEAD >= UNITS):
                        exps(g, m)
                    if n == NC + 1 or n == UNITS - 1:
                        finish(h, slot, 0 if n == NC + 1 else 1)
                    if n == 10 and not isinstance(h, int):
                        split(h + 2, slot)
                    if not last:
                        prepare(h + 1, 1 - slot, n)

            over_heads(act, first, body)

        def mixed(t, h, slot, half):
            x = slice(half * BANK, (half + 1) * BANK)
            if isinstance(h, int):
                return t[NUM[slot], h // 2, x]
            return t[NUM[slot], bass.ds((h - slot) // 2, 1), x].rearrange("p a b -> p (a b)")

        def mla_vector(dve):
            dve.wait_ge(m_rope, 16)
            dve.wait_ge(o_norm, 2 * GH)
            rows, sine = slice(NOPE, QK), slice(QK, P)
            dve.tensor_tensor(k_f[rows, 0:LAT], side_p[rows, 0:LAT], rope[rows], ALU.mult).then_inc(pr_rot, 1)
            dve.tensor_tensor(k_rot[rows], side_p[sine, 0:LAT], rope[sine], ALU.mult).then_inc(pr_rot, 1)
            dve.tensor_copy(k_f[rows, LAT:], side_p[rows, LAT:]).then_inc(pr_rot, 1)
            dve.wait_ge(pr_rot, 3)
            dve.tensor_tensor(k_f[rows, 0:LAT], k_f[rows, 0:LAT], k_rot[rows], ALU.add).then_inc(pr_rot, 1)
            dve.wait_ge(pr_hi, 1)
            dve.tensor_tensor(kvn_lo[:, :], kv_p, kvn_hi[:, :].bitcast(F32), ALU.subtract).then_inc(pr_lo, 1)
            def split(h, slot):
                dve.wait_ge(m_w_hi, h * 2 + 1)
                dve.tensor_tensor(wq_lo[:, slot], wq_raw[:, slot], wq_hi[:, slot].bitcast(F32), ALU.subtract)\
                    .then_inc(m_w_lo, 1)
                dve.wait_ge(m_w_hi, h * 2 + 2)
                dve.tensor_tensor(wkv_lo[:, slot], wkv_raw[:, slot], wkv_hi[:, slot].bitcast(F32), ALU.subtract)\
                    .then_inc(m_w_lo, 1)

            def prepare(h, slot, n):
                two = bank[:, 0:2].rearrange("p a b -> p (a b)")
                if n == KEYS:
                    dve.wait_ge(mk_hi, h + 1)
                    dve.tensor_tensor(k_lo[0:NOPE, slot], bank[0:NOPE, 0:3].rearrange("p a b -> p (a b)")[:, 0:TOK],
                                      k_hi[0:NOPE, slot].bitcast(F32), ALU.subtract).then_inc(mk_lo, 1)
                if n == QUERIES:
                    dve.wait_ge(mq_mm, h + 1)
                    dve.wait_ge(mq_raw, h + 1)
                    dve.wait_ge(mq_lo, h)
                    dve.tensor_tensor(q_f[rows], two[rows], rope[rows], ALU.mult).then_inc(mq_rope, 1)
                    dve.wait_ge(mq_rope, h * 3 + 1)
                    dve.tensor_tensor(two[rows], two[sine], rope[sine], ALU.mult).then_inc(mq_rope, 1)
                    dve.wait_ge(mq_rope, h * 3 + 2)
                    dve.tensor_tensor(q_f[rows], q_f[rows], two[rows], ALU.add).then_inc(mq_rope, 1)
                if n == Q_PARTS:
                    dve.wait_ge(mq_hi, h + 1)
                    dve.tensor_tensor(q_lo[0:QK, slot], q_f[0:QK], q_hi[0:QK, slot].bitcast(F32), ALU.subtract)\
                        .then_inc(mq_lo, 1)
                if n == VALUES:
                    dve.wait_ge(mv_hi, h + 1)
                    cols = slice(VCOL[slot], VCOL[slot] + VD)
                    src = two[:, 0:NC * VD].rearrange("p (t v) -> p t v", v=VD)
                    dve.tensor_tensor(v_lo[:, slot, :, cols], src, v_hi[:, slot, :, cols].bitcast(F32),
                                      ALU.subtract).then_inc(mv_lo, 1)
                if n in COARSE:
                    t = COARSE[n]
                    dve.wait_ge(c_mm, h * QT + (t + 1))
                    at = coarse_bank(h, t)
                    dve.tensor_reduce(row_max[:, t, QK:QK + 1], bank[:, at:at + 3].rearrange("p a b -> p (a b)")[:, 0:TOK],
                                      AX.X, ALU.max).then_inc(c_max, 1)

            def parts(h, n):
                if HI_ON[n] == "dve":
                    dve.wait_ge(s_exp, h * UNITS + (n + 1))
                    dve.tensor_copy(p_hi[:, n % 4], p_f[:, n % 4]).then_inc(part_hi["dve"], 1)
                low(dve, "dve", h, n)

            def gather(h, slot, half):
                a = h * 2 + half
                dve.wait_ge(pv_mm, h * UNITS + (half + 1) * NC)
                dve.wait_ge(acc_lo, a + 1)
                dve.tensor_copy(acc_f[:, :], bank[:, 7]).then_inc(acc_out, 1)

            def finish(h, slot, half):
                a = h * 2 + half
                o = acc_f[NUM[slot]]
                dve.wait_ge(acc_root, a * 2 + 2)
                dve.tensor_tensor(o, o, acc_r[NUM[slot]], ALU.mult).then_inc(acc_div, 1)
                dve.wait_ge(acc_hi, a + 1)
                dve.tensor_tensor(mixed(mix_lo, h, slot, half), o, mixed(mix_hi, h, slot, half).bitcast(F32),
                                  ALU.subtract).then_inc(acc_lo, 1)

            def first():
                split(0, 0)
                split(1, 1)
                dve.wait_ge(pr_khi, 2)
                for slot in range(2):
                    dve.tensor_tensor(k_lo[rows, slot], k_f[rows], k_hi[rows, slot].bitcast(F32), ALU.subtract)\
                        .then_inc(pr_klo, 1)
                dve.wait_ge(pr_hi, 2)
                dve.tensor_tensor(qn_lo[:, :, :], qa_p, qn_hi[:, :, :].bitcast(F32), ALU.subtract).then_inc(pr_lo, 1)
                for n in range(TURN + 1):
                    if n == KEYS + 1 or n == QUERIES + 1:
                        for m in range(GH):
                            gla_low(dve, m if n == KEYS + 1 else m + GH)
                    if n == VALUES:
                        dve.wait_ge(filled, MLA_FILLS)
                    prepare(0, 0, n)
                for n in range(AHEAD):
                    parts(0, n)

            def body(h, slot, last):
                for n in range(UNITS):
                    g, _, m = after(h, slot, n)
                    if n == NC - 1 or n == UNITS - 1:
                        gather(h, slot, n // NC)
                    if not last and n in COARSE:
                        prepare(h + 1, 1 - slot, n)
                    if not (last and n + AHEAD >= UNITS):
                        parts(g, m)
                    if n == NC + 1 or n == UNITS - 1:
                        finish(h, slot, 0 if n == NC + 1 else 1)
                    if n == 10 and not isinstance(h, int):
                        split(h + 2, slot)
                    if not last and n not in COARSE:
                        prepare(h + 1, 1 - slot, n)

            over_heads(dve, first, body)

        def wo_tiles(eng, tile):
            tile(0, 0)
            tile(1, 1)
            with eng.Fori(0, 3) as i:
                for slot in range(2):
                    tile(i * 2 + (2 + slot), slot)

        def wo_sync(sp):
            sp.wait_ge(pv_mm, HEADS * UNITS)
            def load(t, slot):
                if not isinstance(t, int):
                    sp.wait_ge(wo_split_lo, t + (IN_TILES - 1))
                sp.dma_start(wo_raw[:, slot], w_out[bass.ds(t, 1)].rearrange("a p k m -> p (a k) m"))\
                    .then_inc(w_in_sem[slot], 16)

            def loads(t, slot):
                load(t, slot)
                for k in range(4):
                    ada_load(sp, ada_c, t * 4 + k, k)
            ada_cond(sp, ada_c)
            wo_tiles(sp, loads)

        def wo_scalar(act):
            def split(t, slot):
                act.wait_ge(w_in_sem[slot], t * 8 + (16 * 8 + 16 - 8 * slot))
                if not isinstance(t, int) or t >= 2:
                    act.wait_ge(wo_mm, t - 1)
                act.activation(wo_hi[:, slot], wo_raw[:, slot], ACT.Copy).then_inc(wo_split_hi, 1)

            def leave(t, slot):
                act.wait_ge(wo_mm, t + 1)
                act.activation(room2.res[:, bass.ds(t, 1)].rearrange("p a b -> p (a b)"),
                               bank[:, 2 * slot:2 * slot + 2].rearrange("p a b -> p (a b)"), ACT.Copy)\
                    .then_inc(wo_out, 1)

            split(0, 0)
            split(1, 1)
            ada_silu(act, ada_c)
            with act.Fori(0, 3) as i:
                for slot in range(2):
                    leave(i * 2 + slot, slot)
                    split(i * 2 + (2 + slot), slot)
            leave(6, 0)
            leave(7, 1)

        def wo_vector(dve):
            def split(t, slot):
                dve.wait_ge(wo_split_hi, t + (IN_TILES + 1))
                dve.tensor_tensor(wo_lo[:, slot], wo_raw[:, slot], wo_hi[:, slot].bitcast(F32),
                                  ALU.subtract).then_inc(wo_split_lo, 1)

            split(0, 0)
            for n in range(ada_c.tiles):
                if n % 4 == 0 and n // 4 + 1 < DK:
                    split(n // 4 + 1, (n // 4 + 1) % 2)
                ada_tile(dve, ada_c, n)
            ada_finish(dve, ada_c, (2,), (1, 2))

        def wo_tensor(pe):
            pe.wait_ge(acc_lo, 2 * HEADS + 1)
            pe.wait_ge(o_lo, 2 * GH)
            def tile(t, slot):
                pe.wait_ge(wo_split_lo, t + (IN_TILES + 1))
                if not isinstance(t, int):
                    pe.wait_ge(wo_out, t + (IN_TILES - 1))
                for c in range(2):
                    x = slice(c * BANK, (c + 1) * BANK)
                    for k in range(DK):
                        acc = bank[:, 2 * slot + c]
                        pe.matmul(acc, wo_hi[:, slot, k], mix_hi[:, k, x], start=(k == 0), stop=False)
                        pe.matmul(acc, wo_hi[:, slot, k], mix_lo[:, k, x], start=False, stop=False)
                        last = pe.matmul(acc, wo_lo[:, slot, k], mix_hi[:, k, x], start=False, stop=(k == DK - 1))
                last.then_inc(wo_mm, 1)
            wo_tiles(pe, tile)

        def y_added(eng, f):
            def wait(c, k):
                eng.wait_ge(f.y_add, 2 + (PAIRS - 1) * DK * len(f.chunks) + c * DK + k + 1)
            return wait

        @block.sync
        def _(sp):
            ada_cond(sp, ada_a)
            for t in range(4):
                ada_load(sp, ada_a, t, t)
            for t, s in ((bada_sb, b_ada), (pre_sb, pre), (post_sb, post), (ident, ident_d),
                         (mask_raw, mask_d), (wa_sb, w_a), (ba_sb, b_a), (gnorm_sb, g_norm),
                         (qk_norm_sb, qk_norm)):
                sp.dma_start(t[:], s).then_inc(consts_in, 16)
            norm_sync(sp, n1)
            first_load(sp, f1)
            with sp.Fori(0, ada_a.tiles // 4 - 1) as i:
                for k in range(4):
                    ada_load(sp, ada_a, i * 4 + (4 + k), k)

            def loads_b(k):
                if k == 0:
                    sp.wait_ge(n1.lo, DK * 3)
                    ada_cond(sp, ada_b)
                for t in range(*((0, 12), (12, 18), (18, 24))[k]):
                    ada_load(sp, ada_b, t, t % 4)
            ffn_sync(sp, f1, loads_b, early=True)
            norm_sync(sp, n2, lambda: sp.wait_ge(f1.half, 2 * FJ), lambda: proj_first_load(sp))
            sp.wait_ge(n2.stored, 16 * 3)
            proj_sync(sp)
            mla_sync(sp)
            wo_sync(sp)
            sp.wait_ge(acc_lo, 2 * HEADS + 1)

            def loads_f2():
                sp.wait_ge(wo_mm, DK)
                first_load(sp, f2)
            norm_sync(sp, n3, lambda: sp.wait_ge(wo_mm, 1), loads_f2)
            sp.wait_ge(n3.stored, 16 * 2)
            ffn_sync(sp, f2, early=True)
            norm_sync(sp, n4, lambda: sp.wait_ge(f2.half, 2 * FJ))
            sp.wait_ge(n4.stored, 16 * 2)

        @block.gpsimd
        def _(pool):
            pool.memset(ones[:, :], 1.0).then_inc(filled, 1)
            pool.memset(eps[:, :], EPS).then_inc(filled, 1)
            pool.wait_ge(consts_in, CONSTS)
            pool.tensor_copy(mask[:, :, :].rearrange("p l (r c) -> p l r c", c=C),
                             mask_raw[:, :, :].rearrange("p l (r c) -> p l r c", r=1)
                             .to_broadcast([P, LEVELS, BANK // C, C])).then_inc(filled, 1)
            pool.wait_ge(gains_done, 2)
            pool.memset(room1.res[:, :, :], 0.0).then_inc(f1.y_add, 2)
            norm_pool(pool, n2)
            gla_pool(pool)
            mla_pool(pool)
            norm_pool(pool, n3)
            pool.wait_ge(n3.lo, DK * 2)
            pool.wait_ge(n3.stored, 16 * 2)
            pool.memset(room2.res[:, :, :], 0.0).then_inc(f2.y_add, 2)
            norm_pool(pool, n4)

        @block.scalar
        def _(act):
            ada_silu(act, ada_a)
            act.wait_ge(filled, CONST_FILLS)
            norm_scalar(act, n1, early=lambda: first_high(act, f1), late_highs=True)
            ffn_scalar(act, f1, lambda: ada_silu(act, ada_b), early=True)
            norm_scalar(act, n2, y_added(act, f1), lambda: first_two(proj_high, act))
            proj_scalar(act)
            gla_scalar(act)
            mla_scalar(act)
            wo_scalar(act)
            norm_scalar(act, n3, lambda c, k: act.wait_ge(wo_out, IN_TILES + k + 1), lambda: first_high(act, f2))
            ffn_scalar(act, f2, early=True)
            norm_scalar(act, n4, y_added(act, f2))

        @block.tensor
        def _(pe):
            pe.wait_ge(filled, CONST_FILLS)
            norm_tensor(pe, n1)
            ffn_tensor(pe, f1, n2)
            norm_tensor(pe, n2, lambda: pe.wait_ge(f1.y_add, 2 + PAIRS * DK * len(CHUNKS)))
            proj_tensor(pe)
            gla_tensor(pe)
            mla_tensor(pe)
            wo_tensor(pe)
            norm_tensor(pe, n3)
            ffn_tensor(pe, f2, n4)
            norm_tensor(pe, n4, lambda: pe.wait_ge(f2.y_add, 2 + PAIRS * DK * 2))

        @block.vector
        def _(dve):
            dve.wait_ge(consts_in, CONSTS)
            for t in range(ada_a.tiles):
                ada_tile(dve, ada_a, t)
            ada_finish(dve, ada_a, (0,), ())
            first_low(dve, f1)
            norm_vector(dve, n1)
            tiles = iter(range(ada_b.tiles))

            def more(count):
                for _, t in zip(range(count), tiles):
                    ada_tile(dve, ada_b, t)
                    if t == ada_b.tiles - 1:
                        ada_finish(dve, ada_b, (1,), (0,))
            ffn_vector(dve, f1, more, early=True)
            norm_vector(dve, n2, lambda: first_two(proj_low, dve))
            proj_vector(dve)
            gla_vector(dve)
            mla_vector(dve)
            wo_vector(dve)
            norm_vector(dve, n3, lambda: first_low(dve, f2))
            ffn_vector(dve, f2, early=True)
            norm_vector(dve, n4)


ORDER_IN = ["x_t", "cond", "w_ada", "b_ada", "pre", "post", "f1_in", "f1_out", "f2_in", "f2_out", "w_in", "w_a", "b_a",
            "g_norm", "ident", "mask", "w_qb", "w_kvb", "qk_norm", "rope", "w_out"]


def rotated(first):
    c = np.arange(first, first + ROPE)
    return np.concatenate([c[8:16], c[0:8], c[24:32], c[16:24]])


def lay_out(x, c, ctx, c_ctx, w_ada, b_ada, norm_pre, norm_post, ffn1_w_in, ffn1_w_out, ffn2_w_in, ffn2_w_out, w_in,
            mla_q_norm, mla_w_qb, mla_kv_norm, mla_w_kvb, gla_w_a_fwd, gla_b_a_fwd, gla_w_a_bwd, gla_b_a_bwd,
            gla_norm, w_out):
    a = {"x_t": np.concatenate([x[0], ctx[0]]).T.reshape(DK, P, TOK).transpose(1, 0, 2)}
    a["cond"] = np.stack([c[0], c_ctx])
    a["w_ada"] = w_ada[0].T.reshape(9 * DK, P, D)
    a["b_ada"] = np.repeat(b_ada[0].reshape(9, DK, P, 1).transpose(2, 0, 1, 3), 2, -1)
    a["pre"] = np.repeat(norm_pre[0].reshape(3, DK, P, 1).transpose(2, 0, 1, 3), 2, -1)
    a["post"] = np.repeat(norm_post[0].reshape(3, DK, P, 1).transpose(2, 0, 1, 3), 2, -1)
    for f, w1, w2 in (("f1", ffn1_w_in, ffn1_w_out), ("f2", ffn2_w_in, ffn2_w_out)):
        a[f + "_in"] = w1[0].reshape(DK, P, 2, FJ, P).transpose(3, 2, 1, 0, 4).reshape(2 * FJ, P, DK, P)
        a[f + "_out"] = w2[0].reshape(FJ, P, D)
    at = np.cumsum([0, QRANK, KVRANK, ROPE, GH * GDK, GH * GDK, GH * GDV, GH * GDV, 2 * GRANK])
    part = [np.arange(at[i], at[i + 1]) for i in range(8)]
    cols = np.concatenate([part[1], part[7], part[2], part[2], rotated(at[2]), part[4], part[5], part[0], part[3],
                           part[6]])
    a["w_in"] = w_in[0][:, cols].reshape(DK, P, 16, P).transpose(2, 1, 0, 3)
    w_a = np.zeros((2 * GRANK, 4, P), w_in.dtype)
    w_a[:GRANK, 0:2] = gla_w_a_fwd[0].reshape(GRANK, 2, P)
    w_a[GRANK:, 2:4] = gla_w_a_bwd[0].reshape(GRANK, 2, P)
    a["w_a"] = w_a
    a["b_a"] = np.concatenate([gla_b_a_fwd[0], gla_b_a_bwd[0]]).reshape(4, P).T
    a["g_norm"] = gla_norm[0].reshape(P, 1)
    a["ident"] = np.eye(P, dtype=np.float32)
    i = np.arange(C)
    same = np.stack([i[:, None] // b == i[None] // b for b in [C >> k for k in range(1, LEVELS + 1)]], 1)
    a["mask"] = same.astype(np.float32)
    heads = np.concatenate([np.concatenate([np.arange(h * QK, (h + 1) * QK), rotated(h * QK + NOPE)])
                            for h in range(HEADS)])
    a["w_qb"] = mla_w_qb[0][:, heads].reshape(2, P, HEADS, P).transpose(2, 1, 0, 3)
    a["w_kvb"] = mla_w_kvb[0].reshape(P, HEADS, P).transpose(1, 0, 2)
    a["qk_norm"] = np.stack([mla_q_norm[0][:P], mla_q_norm[0][P:], mla_kv_norm[0]], 1)
    a["rope"] = rope_table()
    a["w_out"] = w_out[0].reshape(DK, P, DK, P).transpose(2, 1, 0, 3)
    return {n: np.ascontiguousarray(v) for n, v in a.items()}


def rope_table():
    t = np.arange(LAT, dtype=np.float32)
    freq = (np.float32(10000.0) ** (-np.arange(0, ROPE // 2, 2, dtype=np.float32) / np.float32(ROPE // 2)))
    row, col = np.floor(t / GRID_W).astype(np.float32), (t % GRID_W).astype(np.float32)
    ang = np.concatenate([row * freq[:, None]] * 2 + [col * freq[:, None]] * 2)
    sign = np.where(np.arange(ROPE) % 16 < 8, -1, 1).astype(np.float32)[:, None]
    table = np.zeros((P, LAT), np.float32)
    table[NOPE:QK] = np.cos(ang)
    table[QK:] = np.sin(ang) * sign
    return table


def kernel(**inputs):
    import concourse.bacc as bacc
    from concourse.bass_utils import run_bass_kernel_spmd

    nc = bacc.Bacc("TRN2", target_bir_lowering=False, num_devices=1)
    a = lay_out(**{n: np.asarray(v) for n, v in inputs.items()})
    arrays = {f"in_{n}": a[n] for n in ORDER_IN}
    args = [nc.dram_tensor(n, v.shape, mybir.dt.from_np(v.dtype), kind="ExternalInput").ap()
            for n, v in arrays.items()]
    x1 = nc.dram_tensor("x1", (P, DK, TOK), F32, kind="Internal").ap()
    x2 = nc.dram_tensor("x2", (P, DK, LAT), F32, kind="Internal").ap()
    out = nc.dram_tensor("out", (P, DK, LAT), F32, kind="ExternalOutput").ap()
    build(nc, *args, x1, x2, out)
    r = run_bass_kernel_spmd(nc, [arrays], core_ids=[0])
    y = r.results[0]["out"]
    return y.transpose(1, 0, 2).reshape(D, LAT).T.reshape(1, LAT, D)
```
